# Optimizing a Trainium2 kernel written in Bass

```python
import jax, jax.numpy as jnp
from jax import lax
import numpy as np

D_MODEL = 1024
BATCH = 1
SEQ = 128
DEPTH = 1
DEC_BATCH = 1
DEC_SEQ = 512
PAST_LEN = 256

GRID_W = 64
CONV_WIDTH = 512
CONV_K = 3
NA_HEADS = 8
NA_HEAD_DIM = 64
NA_WIDTH = NA_HEADS * NA_HEAD_DIM
WIN_H = 8
WIN_W = 16
COL_BLOCK = 16
COL_BAND = 32
PEER_HEADS = 8
PEER_KEY_DIM = 256
N_KEYS = 128
N_EXPERTS = N_KEYS * N_KEYS
PEER_TOPK = 16
PEER_BLOCK = 128
LN_EPS = 1e-5
NEG_INF = -1e30
ALPHA = (2 * DEPTH) ** 0.25
BETA = (8 * DEPTH) ** -0.25
IN_COLS = 3 * CONV_WIDTH + 3 * NA_WIDTH + 2 * D_MODEL
IN_SPLITS = (CONV_WIDTH, 2 * CONV_WIDTH, 3 * CONV_WIDTH,
             3 * CONV_WIDTH + NA_WIDTH, 3 * CONV_WIDTH + 2 * NA_WIDTH,
             3 * CONV_WIDTH + 3 * NA_WIDTH, 3 * CONV_WIDTH + 3 * NA_WIDTH + D_MODEL)

kernel_name = "hybrid_flow_shortconv_natten_peer_step"

def layer_norm(x, g, b):
    xf = x.astype(jnp.float32)
    mu = jnp.mean(xf, axis=-1, keepdims=True)
    var = jnp.mean(jnp.square(xf - mu), axis=-1, keepdims=True)
    y = (xf - mu) * lax.rsqrt(var + LN_EPS)
    return y.astype(x.dtype) * g + b

def short_conv(xc, bg, cg, conv_w):
    h = cg * xc
    n = h.shape[1]
    pad = CONV_K // 2
    hp = jnp.pad(h, ((0, 0), (pad, pad), (0, 0)))
    y = conv_w[0] * hp[:, 0:n]
    for i in range(1, CONV_K):
        y = y + conv_w[i] * hp[:, i:i + n]
    return bg * y

def context_attention(q, k, v):
    s = jnp.einsum('bqhd,bkhd->bhqk', q, k).astype(jnp.float32) * (NA_HEAD_DIM ** -0.5)
    p = jax.nn.softmax(s, axis=-1).astype(v.dtype)
    return jnp.einsum('bhqk,bkhd->bqhd', p, v)

def neighbourhood_attention(q, k, v, k_ctx, v_ctx, rpb):
    b, n, h, dh = q.shape
    rows = n // GRID_W
    kh = min(WIN_H, rows)
    n_cb = GRID_W // COL_BLOCK
    r = np.arange(rows)
    row_start = np.clip(r - kh // 2, 0, rows - kh)
    row_idx = row_start[:, None] + np.arange(kh)[None, :]
    col = np.arange(GRID_W)
    col_start = np.clip(col - WIN_W // 2, 0, GRID_W - WIN_W).reshape(n_cb, COL_BLOCK)
    qcol = col.reshape(n_cb, COL_BLOCK)
    band_start = np.clip(np.arange(n_cb) * COL_BLOCK - WIN_W // 2, 0, GRID_W - COL_BAND)
    band_idx = band_start[:, None] + np.arange(COL_BAND)[None, :]
    in_win = ((band_idx[:, None, :] >= col_start[:, :, None]) &
              (band_idx[:, None, :] < col_start[:, :, None] + WIN_W))
    dr = row_idx - r[:, None] + (WIN_H - 1)
    dc = np.clip(band_idx[:, None, :] - qcol[:, :, None], -(WIN_W - 1), WIN_W - 1) + (WIN_W - 1)
    bias = rpb.astype(jnp.float32)[:, dr[:, None, None, :, None], dc[None, :, :, None, :]]
    bias = jnp.where(jnp.asarray(in_win)[None, None, :, :, None, :], bias, NEG_INF)

    qg = q.reshape(b, rows, n_cb, COL_BLOCK, h, dh)
    kg = k.reshape(b, rows, GRID_W, h, dh)
    vg = v.reshape(b, rows, GRID_W, h, dh)
    k_band = kg[:, row_idx][:, :, :, band_idx]
    v_band = vg[:, row_idx][:, :, :, band_idx]
    scale = NA_HEAD_DIM ** -0.5
    s_win = jnp.einsum('brjqhd,brijkhd->bhrjqik', qg, k_band).astype(jnp.float32) * scale + bias[None]
    s_ctx = jnp.einsum('brjqhd,bchd->bhrjqc', qg, k_ctx).astype(jnp.float32) * scale
    n_win = kh * COL_BAND
    s = jnp.concatenate([s_win.reshape(s_win.shape[:5] + (n_win,)), s_ctx], axis=-1)
    p = jax.nn.softmax(s, axis=-1).astype(v.dtype)
    p_win = p[..., :n_win].reshape(s_win.shape)
    p_ctx = p[..., n_win:]
    o = (jnp.einsum('bhrjqik,brijkhd->brjqhd', p_win, v_band) +
         jnp.einsum('bhrjqc,bchd->brjqhd', p_ctx, v_ctx))
    return o.reshape(b, n, h, dh)

def peer(x, w_query, sub_keys, expert_u, expert_v):
    b, n, d = x.shape
    t = b * n
    xt = x.reshape(t, d)
    q = (xt @ w_query).reshape(t, PEER_HEADS, 2, PEER_KEY_DIM // 2)
    s = jnp.einsum('thpd,hpkd->thpk', q, sub_keys).astype(jnp.float32)
    s_half, i_half = lax.top_k(s, PEER_TOPK)
    cand = s_half[:, :, 0, :, None] + s_half[:, :, 1, None, :]
    cand_idx = i_half[:, :, 0, :, None] * N_KEYS + i_half[:, :, 1, None, :]
    top_s, top_pos = lax.top_k(cand.reshape(t, PEER_HEADS, PEER_TOPK * PEER_TOPK), PEER_TOPK)
    experts = jnp.take_along_axis(cand_idx.reshape(t, PEER_HEADS, PEER_TOPK * PEER_TOPK), top_pos, axis=-1)
    gates = jax.nn.softmax(top_s, axis=-1).astype(x.dtype)
    hk = PEER_HEADS * PEER_TOPK
    nb = -(-t // PEER_BLOCK)
    pad = nb * PEER_BLOCK - t
    xb = jnp.pad(xt, ((0, pad), (0, 0))).reshape(nb, PEER_BLOCK, d)
    eb = jnp.pad(experts.reshape(t, hk), ((0, pad), (0, 0))).reshape(nb, PEER_BLOCK, hk)
    gb = jnp.pad(gates.reshape(t, hk), ((0, pad), (0, 0))).reshape(nb, PEER_BLOCK, hk)

    def apply_block(args):
        xs, es, gs = args
        u = expert_u[es]
        vv = expert_v[es]
        a = jax.nn.gelu(jnp.einsum('tkd,td->tk', u, xs), approximate=False)
        return jnp.einsum('tk,tkd->td', gs * a, vv)

    y = lax.map(apply_block, (xb, eb, gb)).reshape(nb * PEER_BLOCK, d)[:t]
    return y.reshape(b, n, d)

def layer(x, cond, k_ctx, v_ctx, w_ada, b_ada, w_in, conv_w, w_conv_out, w_na_out, rpb, w_o,
          ln1_g, ln1_b, w_query, sub_keys, expert_u, expert_v, ln2_g, ln2_b):
    b, n, _ = x.shape
    mods = (jax.nn.silu(cond) @ w_ada + b_ada)[:, None, :]
    sh1, sc1, ga1, sh2, sc2, ga2 = jnp.split(mods, 6, axis=-1)
    u = x * (1 + sc1) + sh1
    xc, bg, cg, q, k, v, g_conv, g_na = jnp.split(u @ w_in, IN_SPLITS, axis=-1)
    y_conv = short_conv(xc, bg, cg, conv_w)
    q = q.reshape(b, n, NA_HEADS, NA_HEAD_DIM)
    k = k.reshape(b, n, NA_HEADS, NA_HEAD_DIM)
    v = v.reshape(b, n, NA_HEADS, NA_HEAD_DIM)
    if k_ctx is None:
        y_na = context_attention(q, k, v)
    else:
        y_na = neighbourhood_attention(q, k, v, k_ctx, v_ctx, rpb)
    y_na = y_na.reshape(b, n, NA_WIDTH)
    merged = (jax.nn.sigmoid(g_conv) * (y_conv @ w_conv_out) +
              jax.nn.sigmoid(g_na) * (y_na @ w_na_out))
    x = layer_norm(ALPHA * x + ga1 * (merged @ w_o), ln1_g, ln1_b)
    u2 = x * (1 + sc2) + sh2
    x = layer_norm(ALPHA * x + ga2 * peer(u2, w_query, sub_keys, expert_u, expert_v), ln2_g, ln2_b)
    return x, k, v

def setup_inputs(seed: int = 0) -> dict:
    key = jax.random.key(seed)
    ks = jax.random.split(key, 24)

    def nrm(k, shape, s):
        return jax.random.normal(k, shape, jnp.float32) * s

    cache_shape = (DEC_BATCH, DEPTH, PAST_LEN, NA_HEADS, NA_HEAD_DIM)
    return {
        'x_prompt': nrm(ks[0], (BATCH, SEQ, D_MODEL), 1.0),
        'x_sample': nrm(ks[1], (DEC_BATCH, DEC_SEQ, D_MODEL), 1.0),
        'cache_k': nrm(ks[2], cache_shape, 1.0),
        'cache_v': nrm(ks[3], cache_shape, 1.0),
        'c': nrm(ks[4], (DEC_BATCH, D_MODEL), 1.0),
        'c_ctx': nrm(ks[5], (D_MODEL,), 1.0),
        'w_ada': nrm(ks[6], (DEPTH, D_MODEL, 6 * D_MODEL), 0.5 * D_MODEL ** -0.5),
        'b_ada': nrm(ks[7], (DEPTH, 6 * D_MODEL), 0.02),
        'w_in': nrm(ks[8], (DEPTH, D_MODEL, IN_COLS), D_MODEL ** -0.5),
        'conv_w': nrm(ks[9], (DEPTH, CONV_K, CONV_WIDTH), CONV_K ** -0.5),
        'w_conv_out': nrm(ks[10], (DEPTH, CONV_WIDTH, D_MODEL), CONV_WIDTH ** -0.5),
        'w_na_out': nrm(ks[11], (DEPTH, NA_WIDTH, D_MODEL), NA_WIDTH ** -0.5),
        'rpb': nrm(ks[12], (DEPTH, NA_HEADS, 2 * WIN_H - 1, 2 * WIN_W - 1), 0.1),
        'w_o': nrm(ks[13], (DEPTH, D_MODEL, D_MODEL), BETA * D_MODEL ** -0.5),
        'ln1_g': 1.0 + nrm(ks[14], (DEPTH, D_MODEL), 0.02),
        'ln1_b': nrm(ks[15], (DEPTH, D_MODEL), 0.02),
        'w_query': nrm(ks[16], (DEPTH, D_MODEL, PEER_HEADS * PEER_KEY_DIM), D_MODEL ** -0.5),
        'sub_keys': nrm(ks[17], (DEPTH, PEER_HEADS, 2, N_KEYS, PEER_KEY_DIM // 2), (PEER_KEY_DIM // 2) ** -0.5),
        'expert_u': nrm(ks[18], (DEPTH, N_EXPERTS, D_MODEL), D_MODEL ** -0.5),
        'expert_v': nrm(ks[19], (DEPTH, N_EXPERTS, D_MODEL), BETA),
        'ln2_g': 1.0 + nrm(ks[20], (DEPTH, D_MODEL), 0.02),
        'ln2_b': nrm(ks[21], (DEPTH, D_MODEL), 0.02),
    }

def reference(x_prompt, x_sample, cache_k, cache_v, c, c_ctx, w_ada, b_ada, w_in, conv_w,
              w_conv_out, w_na_out, rpb, w_o, ln1_g, ln1_b, w_query, sub_keys, expert_u,
              expert_v, ln2_g, ln2_b):
    h_ctx = x_prompt
    h_lat = x_sample
    new_k, new_v = [], []
    for l in range(DEPTH):
        params = (w_ada[l], b_ada[l], w_in[l], conv_w[l], w_conv_out[l], w_na_out[l], rpb[l],
                  w_o[l], ln1_g[l], ln1_b[l], w_query[l], sub_keys[l], expert_u[l], expert_v[l],
                  ln2_g[l], ln2_b[l])
        h_ctx, k_l, v_l = layer(h_ctx, c_ctx[None, :], None, None, *params)
        new_k.append(k_l)
        new_v.append(v_l)
        h_lat, _, _ = layer(h_lat, c, cache_k[:, l], cache_v[:, l], *params)
    new_cache_k = jnp.stack(new_k, axis=1)
    new_cache_v = jnp.stack(new_v, axis=1)
    return (h_ctx, h_lat, new_cache_k, new_cache_v)


_drawn_inputs = setup_inputs


def setup_inputs(seed=0):
    import zlib

    import numpy as np

    out = dict(_drawn_inputs(seed))
    spreads = {}
    factors = {'cache_k': 7.762, 'cache_v': 6.773, 'rpb': 64.0, 'ln2_g': 8.702, 'ln2_b': 8.108}
    for name, (base, spread) in spreads.items():
        noise = np.random.default_rng([zlib.crc32(name.encode()), seed]).standard_normal(out[name].shape)
        drawn = base * np.exp(spread * noise) if base else spread * noise
        out[name] = __import__('jax').numpy.asarray(drawn.astype(out[name].dtype))
    for name, factor in factors.items():
        out[name] = (out[name] * factor).astype(out[name].dtype)
    return out
```

```python
from contextlib import ExitStack

import numpy as np

import concourse.bass as bass
from concourse import mybir

ALU = mybir.AluOpType
ACT = mybir.ActivationFunctionType
AX = mybir.AxisListType.X
F32 = mybir.dt.float32
U32 = mybir.dt.uint32

P = 128
D = 1024
KD = D // P
CTX, LAT = 128, 512
NT = CTX + LAT
TILES = NT // P
SECTIONS = ((0, CTX), (CTX, LAT))
GRID_W, ROWS = 64, 8
PAST = 256
HEADS, HD = 8, 64
WIN_W, COL_BLOCK, COL_BAND = 16, 16, 32
WIDE = COL_BLOCK + COL_BAND
BLOCKS = GRID_W // COL_BLOCK
RPB_H, RPB_W = 15, 31
PEER_HEADS, TOPK, NKEYS = 8, 16, 128
HK = PEER_HEADS * TOPK
CAND = TOPK * TOPK
GROUP = 8
GROUPS = HK // GROUP
SCALE = HD ** -0.5
ALPHA = 2.0 ** 0.25
EPS = 1e-5
NEG = -1e30
LOWEST = -3.0e38
HALF = 512
WSLOTS = 3

BAND_START = [min(max(j * COL_BLOCK - WIN_W // 2, 0), GRID_W - COL_BAND) for j in range(BLOCKS)]
MASK_OF = [0, 1, 1, 2]


def window_mask():
    m = np.zeros((P, 3, COL_BAND), np.float32)
    for j in (0, 1, 3):
        for p in range(P):
            q = j * COL_BLOCK + p % COL_BLOCK
            start = min(max(q - WIN_W // 2, 0), GRID_W - WIN_W)
            cols = BAND_START[j] + np.arange(COL_BAND)
            m[p, MASK_OF[j], (cols < start) | (cols >= start + WIN_W)] = NEG
    return m.reshape(P, 3 * COL_BAND)


def weight_loads():
    loads = [("ada", g) for g in range(4)]
    for n, g in enumerate(PROJ):
        loads.append(("in", g))
        if n < 4:
            loads += [("ada", 4 + 2 * n), ("ada", 5 + 2 * n)]
    loads.append(("in", 5))
    for s in range(2):
        for hf in range(2):
            loads += [("gconv", s, hf), ("gna", s, hf), ("branch", s, hf)]
        loads += [("out", s, 0), ("out", s, 1)]
        loads += [("query", s, g) for g in range(4)]
    return loads


PROJ = (0, 2, 1, 3, 4)


def mod_adds(g):
    return g + 1 if g < 4 else g + 2


def units():
    out = [("ctx", b, 0, 0) for b in range(2)]
    out += [("lat", hp, j, par) for hp in range(HEADS // 2) for j in range(BLOCKS) for par in range(2)]
    return out


UNITS = units()
NU = len(UNITS)


def exps_upto(n):
    return 4 * (n + 1) if n < 2 else 8 + (n - 1)


def outputs_upto(n):
    return n + 1 if n < 2 else 2 + (n - 1) // 2


def out_block(n):
    return n if n < 2 else 2 + (n - 2) // 2


def backbone(nc, x_prompt, x_sample, xT, ck_T, cache_v, c_T, w_ada, b_ada, w_in, convw_T, w_conv_out,
             w_na_out, rpb_rows, w_o, ln1_g, ln1_b, w_query, sub_keys_T, expert_u, expert_v, ln2_g, ln2_b,
             ident_in, mask_in, iota_in, y_prompt, y_sample, new_k, new_v):
    mods_d = nc.dram_tensor("mods_d", (2, 6 * D), F32, kind="Internal").ap()
    x1_d = nc.dram_tensor("x1_d", (NT, D), F32, kind="Internal").ap()
    u2_d = nc.dram_tensor("u2_d", (NT, D), F32, kind="Internal").ap()

    def rows(prompt, sample, e):
        return prompt[0] if e == 0 else sample[0, (e - 1) * P:e * P, :]

    with ExitStack() as ctx:
        def sem(name):
            return ctx.enter_context(nc.semaphore(name))

        arena = ctx.enter_context(nc.sbuf_tensor("arena", [P, 52736], F32))
        psum = ctx.enter_context(nc.psum_tensor("psum", [P, 8 * HALF], F32))

        def bank(b, n=1):
            return psum[:, b * HALF:(b + n) * HALF]

        def at(off, *shape):
            n = int(np.prod(shape))
            v = arena[:, off:off + n]
            if len(shape) == 2:
                v = v.rearrange("p (a b) -> p a b", b=shape[1])
            if len(shape) == 3:
                v = v.rearrange("p (a b c) -> p a b c", b=shape[1], c=shape[2])
            return v

        W = [at(4096 * i, KD, HALF) for i in range(WSLOTS)]
        UT = at(12288, KD, NT)
        Aq, Bk, Cy = at(17408, 4, NT), at(19968, 4, NT), at(22528, 4, NT)
        MT = at(17408, KD, LAT)
        V = at(25088, TILES, HALF)
        VB = at(27648, 2 * BLOCKS, HALF)
        MODS = at(27648, 6 * D)[0:2, :]
        SG = [at(27648 + 1024 * i, 2, HALF) for i in range(2)]
        XB = [at(29696 + 1024 * i, D) for i in range(2)]
        CK = at(31744, 4, PAST)
        CV = at(32768, 2, HALF)
        XR = [at(31744 + 1024 * i, D) for i in range(2)]
        WB = at(33792, HEADS, ROWS, WIDE)
        U2 = [at(33792 + 1024 * i, D) for i in range(2)]
        YNA = at(36864, 4, NT)
        CT = at(36864, 4, NT)
        S = [at(39424 + HALF * i, HALF) for i in range(3)]
        PT = [at(40960 + HALF * i, HALF) for i in range(2)]
        PRM = [at(o, D) for o in (25088, 26112, 39424, 40448, 35840)]
        SK = at(41984, 2 * PEER_HEADS, NKEYS)
        QT = at(44032, 4, LAT)
        CANDS = at(27648, PEER_HEADS, CAND)
        EQ = at(29696, PEER_HEADS, CAND)
        IDN = at(46080, P)
        ZERO = at(46208, HALF)
        VAL = at(46720, TILES, 2 * PEER_HEADS * TOPK)
        IDX = at(48000, 2 * PEER_HEADS * TOPK).bitcast(U32)
        IDXF = at(48256, 2 * PEER_HEADS * TOPK)
        EID = at(48512, TILES, HK).bitcast(U32)
        GATE = at(49152, TILES, HK)
        MODT = at(49792, 16, 2)
        CONVW = at(49824, 4, 3)
        MASK = at(49836, 3, COL_BAND)
        IOTA = at(49932, TOPK)
        CT2 = at(49948, KD, 2)
        SIL = at(49964, KD, 2)
        NMAX = at(49980, 3, 4)
        RSUM = at(49992, 3, 4)
        RINV = at(50004, 3, 4)
        STAT = at(50016, 12)
        MV = at(50028, 2)
        RSTD = at(50030, 2)
        SMAX = at(50032, HK)
        AF = at(50160, HK)
        BF = at(50288, HK)
        POS = at(50416, HK).bitcast(U32)
        TOPS = at(50544, PEER_HEADS, TOPK)
        GSUM = at(50672, PEER_HEADS)
        DOT = at(50680, GROUP)
        GEL = at(50688, GROUP)
        WGT = at(50696, GROUP)
        RING = at(50704, GROUP).bitcast(U32)
        PA = at(50712, HK).bitcast(U32)
        PB = at(50840, HK).bitcast(U32)
        SW = at(50968, 4, NKEYS)
        KTOK = at(51480, HALF)
        I0 = at(51992, HK)
        I1 = at(52120, HK)
        UR = [at(1024 * i, D) for i in range(GROUP)]
        VR = [at(8192 + 1024 * i, D) for i in range(GROUP)]
        DG = [at(16384 + P * i, P) for i in range(GROUP)]
        U2B = [at(17408 + 1024 * i, D) for i in range(2)]
        X1B = [at(19456 + 1024 * i, D) for i in range(2)]
        PRM2 = [at(21504 + 1024 * i, D) for i in range(3)]
        YR = [at(25088 + 1024 * i, D) for i in range(2)]

        w_land = [sem(f"w_land{i}") for i in range(WSLOTS)]
        consts_in, x_in, bias_in, ctx_in = sem("consts_in"), sem("x_in"), sem("bias_in"), sem("ctx_in")
        bada_in, keys_in = sem("bada_in"), sem("keys_in")
        silu_step, ada_done, mod_added, modt_done, modt_ready = (
            sem("silu_step"), sem("ada_done"), sem("mod_added"), sem("modt_done"), sem("modt_ready"))
        u_ready, mods_out = sem("u_ready"), sem("mods_out")
        proj_done, proj_out, conv_step = sem("proj_done"), sem("proj_out"), sem("conv_step")
        kt_done, kt_out, cache_out, band_in = sem("kt_done"), sem("kt_out"), sem("cache_out"), sem("band_in")
        sc_done, s_scaled, win_step, max_done, exp_done = (
            sem("sc_done"), sem("s_scaled"), sem("win_step"), sem("max_done"), sem("exp_done"))
        recip_done, norm_done, pt_done, pt_out, pv_done, po_out = (
            sem("recip_done"), sem("norm_done"), sem("pt_done"), sem("pt_out"), sem("pv_done"), sem("po_out"))
        gates_done, merge_done, sig_out, merge_step = (
            sem("gates_done"), sem("merge_done"), sem("sig_out"), sem("merge_step"))
        prm_in = [sem("prm_in0"), sem("prm_in1")]
        xb_in = [sem("xb_in0"), sem("xb_in1")]
        store_out = [sem("store_out0"), sem("store_out1")]
        wo_done, ln_step, sqrt_done, ut_done, ut_out = (
            sem("wo_done"), sem("ln_step"), sem("sqrt_done"), sem("ut_done"), sem("ut_out"))
        q_done, q_out, ss_done, topk_step, pick_step, gexp_done = (
            sem("q_done"), sem("q_out"), sem("ss_done"), sem("topk_step"), sem("pick_step"), sem("gexp_done"))
        tile_in = [sem("tile_in0"), sem("tile_in1")]
        prm2_in, u_land, v_land = sem("prm2_in"), [sem(f"u_land{i}") for i in range(GROUP)], [
            sem(f"v_land{i}") for i in range(GROUP)]
        ring_ready, u_free, v_free, gelu_done, w_ready, diag_ready = (
            sem("ring_ready"), sem("u_free"), sem("v_free"), sem("gelu_done"), sem("w_ready"), sem("diag_ready"))
        zero_set, y_done, fin_step, fsqrt_done = (
            sem("zero_set"), sem("y_done"), sem("fin_step"), sem("fsqrt_done"))
        y_out = [sem("y_out0"), sem("y_out1")]

        loads = weight_loads()
        slot_of = {key: n % WSLOTS for n, key in enumerate(loads)}
        counts, landed = [0] * WSLOTS, {}
        for n, key in enumerate(loads):
            counts[n % WSLOTS] += 32 if key[0] == "branch" else 16
            landed[key] = counts[n % WSLOTS]

        def freed_by(key):
            kind = key[0]
            if kind == "ada":
                return ada_done, key[1] + 1
            if kind == "in":
                return proj_done, 4 * (PROJ.index(key[1]) + 1) if key[1] != 5 else 20 + TILES
            if kind in ("gconv", "gna", "branch"):
                return merge_done, 8 * key[1] + 4 * key[2] + 4
            if kind == "out":
                return wo_done, 1 if key[1] == 0 else TILES
            return q_done, 16 * key[1] + 4 * key[2] + 4

        def weights(pe, key):
            pe.wait_ge(w_land[slot_of[key]], landed[key])
            return W[slot_of[key]]

        def w_cols(w, c0, n=HALF):
            return w[:, c0:c0 + n].rearrange("(k p) n -> p k n", p=P)

        def all_stored(eng):
            for i in range(2):
                eng.wait_ge(store_out[i], 32 * len(range(i, TILES, 2)))

        block = ctx.enter_context(nc.Block())

        @block.sync
        def _(sp):
            for n, key in enumerate(loads):
                if n >= WSLOTS:
                    sp.wait_ge(*freed_by(loads[n - WSLOTS]))
                dst, done = W[n % WSLOTS], w_land[n % WSLOTS]
                kind = key[0]
                if kind == "ada":
                    sp.dma_start(dst, w_cols(w_ada[0], key[1] * HALF)).then_inc(done, 16)
                elif kind == "in":
                    sp.dma_start(dst, w_cols(w_in[0], key[1] * HALF)).then_inc(done, 16)
                elif kind == "gconv":
                    sp.dma_start(dst, w_cols(w_in[0], (6 + key[2]) * HALF)).then_inc(done, 16)
                elif kind == "gna":
                    sp.dma_start(dst, w_cols(w_in[0], (8 + key[2]) * HALF)).then_inc(done, 16)
                elif kind == "branch":
                    sp.dma_start(dst[:, 0:4, :], w_cols(w_conv_out[0], key[2] * HALF)).then_inc(done, 16)
                    sp.dma_start(dst[:, 4:8, :], w_cols(w_na_out[0], key[2] * HALF)).then_inc(done, 16)
                elif kind == "out":
                    sp.dma_start(dst, w_cols(w_o[0], key[2] * HALF)).then_inc(done, 16)
                else:
                    sp.dma_start(dst, w_cols(w_query[0], key[2] * HALF)).then_inc(done, 16)

            sp.wait_ge(pick_step, PICKS * TILES)
            sp.dma_start(PRM2[1], ln2_g[0:1, :].partition_broadcast(P)).then_inc(prm2_in, 16)
            sp.dma_start(PRM2[2], ln2_b[0:1, :].partition_broadcast(P)).then_inc(prm2_in, 16)
            sp.dma_start(PRM2[0], mods_d[0:1, 5 * D:6 * D].partition_broadcast(P)).then_inc(prm2_in, 16)
            all_stored(sp)
            for e in range(TILES):
                if e >= 2:
                    sp.wait_ge(fin_step, FIN * (e - 1))
                sp.dma_start(U2B[e % 2], u2_d[e * P:(e + 1) * P, :]).then_inc(tile_in[e % 2], 16)
                sp.dma_start(X1B[e % 2], x1_d[e * P:(e + 1) * P, :]).then_inc(tile_in[e % 2], 16)
                if e >= 1:
                    sp.wait_ge(fin_step, FIN * e)
                    sp.dma_start(rows(y_prompt, y_sample, e - 1), YR[(e - 1) % 2]).then_inc(y_out[(e - 1) % 2], 16)
                if e == 1:
                    sp.dma_start(PRM2[0], mods_d[1:2, 5 * D:6 * D].partition_broadcast(P)).then_inc(prm2_in, 16)
            sp.wait_ge(fin_step, FIN * TILES)
            sp.dma_start(rows(y_prompt, y_sample, TILES - 1), YR[(TILES - 1) % 2]).then_inc(y_out[(TILES - 1) % 2], 16)
            for i in range(2):
                sp.wait_ge(y_out[i], 16 * len(range(i, TILES, 2)))
            sp.wait_ge(cache_out, 32)

        def store_tile(pool, e):
            pool.wait_ge(ln_step, LNS * (e + 1))
            pool.dma_start(x1_d[e * P:(e + 1) * P, :], XR[e % 2]).then_inc(store_out[e % 2], 16)
            pool.dma_start(u2_d[e * P:(e + 1) * P, :], U2[e % 2]).then_inc(store_out[e % 2], 16)

        @block.gpsimd
        def _(pool):
            pool.dma_start(CT2, c_T).then_inc(consts_in, 16)
            pool.dma_start(IDN, ident_in).then_inc(consts_in, 16)
            pool.dma_start(MODS, b_ada[0:1, :].partition_broadcast(2)).then_inc(bada_in, 16)
            for k in range(KD):
                pool.dma_start(UT[:, k, :], xT[k * P:(k + 1) * P, :]).then_inc(x_in, 16)
            pool.dma_start(CONVW, convw_T).then_inc(consts_in, 16)
            pool.dma_start(MASK, mask_in.rearrange("p (a b) -> p a b", b=COL_BAND)).then_inc(consts_in, 16)
            pool.dma_start(IOTA, iota_in).then_inc(consts_in, 16)
            pool.dma_start(SK, sub_keys_T).then_inc(keys_in, 16)
            length = rpb_rows.shape[1]
            for r in range(ROWS):
                for h in range(HEADS):
                    src = bass.AP(rpb_rows.tensor, h * RPB_H * RPB_W + (ROWS - 1 - r) * RPB_W,
                                  [[length, COL_BLOCK], [RPB_W, ROWS], [1, WIDE]])
                    pool.dma_start(WB[r * COL_BLOCK:(r + 1) * COL_BLOCK, h], src).then_inc(bias_in, 16)
            pool.wait_ge(mod_added, 14)
            pool.dma_start(mods_d, MODS).then_inc(mods_out, 16)
            pool.wait_ge(mods_out, 16)
            for t in range(2):
                pool.dma_start(CV[:, t, :], cache_v[0, 0, t * P:(t + 1) * P].rearrange("t h d -> t (h d)")
                               ).then_inc(ctx_in, 16)
            for c in range(4):
                pool.dma_start(CK[:, c, :], ck_T[c * P:(c + 1) * P, :]).then_inc(ctx_in, 16)
            pool.wait_ge(proj_out, 20 + TILES)
            for j in range(BLOCKS):
                for i in range(ROWS):
                    p0 = (i % 2) * GRID_W + BAND_START[j]
                    pool.dma_start(VB[(i % 4) * COL_BAND:(i % 4 + 1) * COL_BAND, 2 * j + i // 4, :],
                                   V[p0:p0 + COL_BAND, 1 + i // 2, :]).then_inc(band_in, 16)
            pool.dma_start(new_v[0, 0].rearrange("t h d -> t (h d)"), V[:, 0, :]).then_inc(cache_out, 16)
            pool.wait_ge(kt_out, 1)
            pool.dma_start(new_k[0, 0].rearrange("t h d -> t (h d)"), KTOK).then_inc(cache_out, 16)

            pool.wait_ge(po_out, outputs_upto(NU - 1))
            pool.wait_ge(band_in, 16 * BLOCKS * ROWS)
            pool.wait_ge(cache_out, 32)
            for s in range(2):
                if s == 1:
                    pool.wait_ge(ln_step, LNS)
                pool.dma_start(PRM[0], mods_d[s:s + 1, 2 * D:3 * D].partition_broadcast(P)).then_inc(prm_in[s], 16)
                pool.dma_start(PRM[4], mods_d[s:s + 1, 3 * D:4 * D].partition_broadcast(P)).then_inc(prm_in[s], 16)
                pool.dma_start(PRM[3], mods_d[s:s + 1, 4 * D:5 * D].partition_broadcast(P)).then_inc(prm_in[s], 16)
                if s == 0:
                    pool.dma_start(PRM[1], ln1_g[0:1, :].partition_broadcast(P)).then_inc(prm_in[s], 16)
                    pool.dma_start(PRM[2], ln1_b[0:1, :].partition_broadcast(P)).then_inc(prm_in[s], 16)
                else:
                    pool.wait_ge(pick_step, PICKS)
                for e in ((0,) if s == 0 else (1, 2, 3, 4)):
                    if e >= 3:
                        pool.wait_ge(ln_step, LNS * (e - 1))
                    pool.dma_start(XB[e % 2], rows(x_prompt, x_sample, e)).then_inc(xb_in[e % 2], 16)
                    if e >= 2:
                        store_tile(pool, e - 1)
                store_tile(pool, 0 if s == 0 else TILES - 1)

            pool.wait_ge(pick_step, PICKS * TILES)
            pool.wait_ge(q_out, 32)
            all_stored(pool)
            for e in range(TILES):
                with pool.Fori(0, GROUPS) as g:
                    for hb in range(2):
                        first = GROUP * GROUPS * e + GROUP * g + (GROUP // 2) * hb
                        pool.wait_ge(u_free, first + GROUP // 2)
                        pool.wait_ge(v_free, first + GROUP // 2)
                        own = slice((GROUP // 2) * hb, (GROUP // 2) * (hb + 1))
                        pool.tensor_copy(RING[:, own], EID[:, e, bass.ds(GROUP * g + (GROUP // 2) * hb, GROUP // 2)]
                                         ).then_inc(ring_ready, 1)
                        pool.wait_ge(ring_ready, 1)
                        pool.sem_clear(ring_ready)
                        for b in range(own.start, own.stop):
                            pool.indirect_dma_start(UR[b], None, expert_u[0], bass.IndirectOffsetOnAxis(
                                ap=RING[:, b:b + 1], axis=0)).then_inc(u_land[b], 16)
                        for b in range(own.start, own.stop):
                            pool.indirect_dma_start(VR[b], None, expert_v[0], bass.IndirectOffsetOnAxis(
                                ap=RING[:, b:b + 1], axis=0)).then_inc(v_land[b], 16)

        @block.tensor
        def _(pe):
            def ada(g):
                w = weights(pe, ("ada", g))
                if g >= 2:
                    pe.wait_ge(mod_added, mod_adds(g - 2))
                for k in range(KD):
                    mm = pe.matmul(bank(6 + g % 2)[0:2, :], SIL[:, k, :], w[:, k, :], start=k == 0, stop=k == KD - 1)
                mm.then_inc(ada_done, 1)

            def project(n):
                w = weights(pe, ("in", PROJ[n]))
                for c in range(4):
                    i = 4 * n + c
                    if i >= 2:
                        pe.wait_ge(proj_out, i - 1)
                    for k in range(KD):
                        for hf in range(2):
                            mm = pe.matmul(bank(2 * (i % 2) + hf)[:, 0:NT // 2], w[:, k, c * P:(c + 1) * P],
                                           UT[:, k, hf * (NT // 2):(hf + 1) * (NT // 2)],
                                           start=k == 0, stop=k == KD - 1)
                    mm.then_inc(proj_done, 1)

            pe.wait_ge(silu_step, 2)
            for g in range(4):
                ada(g)
            pe.wait_ge(mod_added, 5)
            pe.wait_ge(consts_in, 80)
            for m in range(16):
                mm = pe.transpose(bank(5)[:, 2 * m:2 * m + 2], MODS[:, m * P:(m + 1) * P], IDN[0:2, 0:2])
            mm.then_inc(modt_done, 1)
            pe.wait_ge(u_ready, 16)
            for n in range(5):
                project(n)
                if n < 4:
                    ada(4 + 2 * n)
                    ada(5 + 2 * n)
            w = weights(pe, ("in", 5))
            for t in range(TILES):
                pe.wait_ge(proj_out, 20 + t - 1)
                for k in range(KD):
                    mm = pe.matmul(bank(2 * (t % 2)), UT[:, k, t * P:(t + 1) * P], w[:, k, :], start=k == 0,
                                   stop=k == KD - 1)
                mm.then_inc(proj_done, 1)
            for c in range(4):
                mm = pe.transpose(bank(4)[:, c * P:(c + 1) * P], Bk[:, c, 0:CTX], IDN)
            mm.then_inc(kt_done, 1)

            def scores(n):
                kind, a, j, par = UNITS[n]
                out = bank(n % 2)
                if n == 0:
                    pe.wait_ge(proj_out, 20 + TILES)
                if n >= 2:
                    pe.wait_ge(s_scaled, n - 1)
                if n >= 4:
                    pe.wait_ge(win_step, 2 * (n - 3))
                if kind == "ctx":
                    for i in range(4):
                        p = slice(HD * a, HD * a + HD)
                        mm = pe.matmul(out[:, i * P:(i + 1) * P], Aq[p, i, 0:CTX], Bk[p, i, 0:CTX],
                                       start=True, stop=True)
                else:
                    if n == 2:
                        pe.wait_ge(ctx_in, 96)
                    p = slice(HD * par, HD * par + HD)
                    q = Aq[p, a, CTX + j * P:CTX + (j + 1) * P]
                    k = Bk[p, a, CTX:NT].rearrange("p (r c) -> p r c", c=GRID_W)[:, :, BAND_START[j]:BAND_START[j] + COL_BAND]
                    pe.matmul(out[:, 0:PAST].rearrange("p (r c) -> p r c", c=COL_BAND), q, k, start=True, stop=True)
                    mm = pe.matmul(bank(6 + n % 2)[:, 0:PAST], q, CK[p, a, :], start=True, stop=True)
                mm.then_inc(sc_done, 1)

            def turn(n):
                pe.wait_ge(norm_done, exps_upto(n))
                if n >= 2:
                    pe.wait_ge(pt_out, n - 1)
                for i in range(4):
                    mm = pe.transpose(bank(2 + n % 2)[:, i * P:(i + 1) * P], S[n % 3][:, i * P:(i + 1) * P], IDN)
                mm.then_inc(pt_done, 1)

            def mix(n):
                kind, a, j, par = UNITS[n]
                o = out_block(n)
                pe.wait_ge(pt_out, n + 1)
                if o >= 2:
                    pe.wait_ge(po_out, o - 1)
                if n == 0:
                    pe.wait_ge(kt_out, 1)
                out = bank(4 + o % 2)
                if kind == "ctx":
                    for i in range(4):
                        h = 2 * i + a
                        mm = pe.matmul(out[HD * a:HD * a + HD, i * P:(i + 1) * P],
                                       V[:, 0, h * HD:(h + 1) * HD], PT[n % 2][:, i * P:(i + 1) * P],
                                       start=True, stop=True)
                else:
                    if n == 2:
                        pe.wait_ge(band_in, 16 * BLOCKS * ROWS)
                    h = 2 * a + par
                    for i in range(4):
                        v = VB[:, 2 * j + i, h * HD:(h + 1) * HD] if i < 2 else CV[:, i - 2, h * HD:(h + 1) * HD]
                        mm = pe.matmul(out[HD * par:HD * par + HD, 0:P], v, PT[n % 2][:, i * P:(i + 1) * P],
                                       start=i == 0, stop=i == 3)
                mm.then_inc(pv_done, 1)

            for n in range(NU + 2):
                if n < NU:
                    scores(n)
                if 1 <= n <= NU:
                    turn(n - 1)
                if n >= 2:
                    mix(n - 2)

            pe.wait_ge(po_out, outputs_upto(NU - 1))
            for s, (t0, n_tok) in enumerate(SECTIONS):
                tok = slice(t0, t0 + n_tok)
                if s == 1:
                    pe.wait_ge(topk_step, 80)
                for hf in range(2):
                    wc, wn, wb = (weights(pe, (kind, s, hf)) for kind in ("gconv", "gna", "branch"))
                    for c in range(4):
                        d = 8 * s + 4 * hf + c
                        if 8 * s + 4 * hf + c >= 2:
                            pe.wait_ge(merge_step, 2 * (d - 1))
                        col = slice(c * P, (c + 1) * P)
                        b0 = 4 * (d % 2)
                        for k in range(KD):
                            pe.matmul(bank(b0)[:, 0:n_tok], wc[:, k, col], UT[:, k, tok], start=k == 0, stop=k == KD - 1)
                        for k in range(KD):
                            mm = pe.matmul(bank(b0 + 1)[:, 0:n_tok], wn[:, k, col], UT[:, k, tok], start=k == 0,
                                           stop=k == KD - 1)
                        mm.then_inc(gates_done, 1)
                        for k in range(4):
                            pe.matmul(bank(b0 + 2)[:, 0:n_tok], wb[:, k, col], Cy[:, k, tok], start=k == 0, stop=k == 3)
                        for k in range(4):
                            mm = pe.matmul(bank(b0 + 3)[:, 0:n_tok], wb[:, 4 + k, col], YNA[:, k, tok], start=k == 0,
                                           stop=k == 3)
                        mm.then_inc(merge_done, 1)
                pe.wait_ge(merge_step, 16 * (s + 1))
                w0, w1 = weights(pe, ("out", s, 0)), weights(pe, ("out", s, 1))
                tiles = (0,) if s == 0 else (1, 2, 3, 4)

                def turn_u2(e):
                    pe.wait_ge(ln_step, LNS * (e + 1))
                    if e >= 2:
                        pe.wait_ge(ut_out, e - 1)
                    for k in range(KD):
                        mm = pe.transpose(bank(4 + 2 * (e % 2), 2)[:, k * P:(k + 1) * P],
                                          U2[e % 2][:, k * P:(k + 1) * P], IDN)
                    mm.then_inc(ut_done, 1)

                for e in tiles:
                    loc = slice((e - tiles[0]) * P, (e - tiles[0] + 1) * P)
                    if e >= 3:
                        pe.wait_ge(ln_step, LNS * (e - 2) + 1)
                    for hf, w in enumerate((w0, w1)):
                        for k in range(KD):
                            mm = pe.matmul(bank(2 * (e % 2) + hf), MT[:, k, loc], w[:, k, :], start=k == 0,
                                           stop=k == KD - 1)
                    mm.then_inc(wo_done, 1)
                    if e > tiles[0]:
                        turn_u2(e - 1)
                turn_u2(tiles[-1])
                pe.wait_ge(ut_out, tiles[-1] + 1)
                pe.wait_ge(keys_in, 16)
                for qg in range(4):
                    w = weights(pe, ("query", s, qg))
                    for c in range(4):
                        f = 16 * s + 4 * qg + c
                        if f >= 2:
                            pe.wait_ge(q_out, f - 1)
                        for k in range(KD):
                            mm = pe.matmul(bank(f % 2)[:, 0:n_tok], w[:, k, c * P:(c + 1) * P], UT[:, k, tok],
                                           start=k == 0, stop=k == KD - 1)
                        mm.then_inc(q_done, 1)
                    pe.wait_ge(q_out, 16 * s + 4 * qg + 4)
                    for tl in range(len(tiles)):
                        si = qg if s == 0 else 4 + 4 * qg + tl
                        if si >= 2:
                            pe.wait_ge(topk_step, 20 * (si - 1))
                        for c in range(4):
                            mm = pe.matmul(bank(2 + si % 2)[:, c * P:(c + 1) * P], QT[:, c, tl * P:(tl + 1) * P],
                                           SK[:, 4 * qg + c, :], start=True, stop=True)
                        mm.then_inc(ss_done, 1)

            pe.wait_ge(zero_set, 1)
            for e in range(TILES):
                y = bank(4 + 2 * (e % 2), 2)
                if e >= 2:
                    pe.wait_ge(fin_step, FIN * (e - 2) + 1)
                for hf in range(2):
                    mm = pe.matmul(y[:, hf * HALF:(hf + 1) * HALF], ZERO[:, 0:P], ZERO, start=True, stop=False)
                if e == 0:
                    mm.then_inc(v_free, GROUP)
                with pe.Fori(0, GROUPS) as g:
                    for b in range(GROUP):
                        pe.wait_ge(v_land[b], 16 * GROUPS * e + 16 * g + 16)
                        pe.wait_ge(diag_ready, HK * e + GROUP * g + (b + 1))
                        for hf in range(2):
                            mm = pe.matmul(y[:, hf * HALF:(hf + 1) * HALF], DG[b], VR[b][:, hf * HALF:(hf + 1) * HALF],
                                           start=False, stop=False)
                        mm.then_inc(v_free, 1)
                for hf in range(2):
                    mm = pe.matmul(y[:, hf * HALF:(hf + 1) * HALF], ZERO[:, 0:P], ZERO, start=False, stop=True)
                mm.then_inc(y_done, 1)

        @block.scalar
        def _(act):
            act.wait_ge(consts_in, 80)
            act.activation(SIL, CT2, ACT.Sigmoid).then_inc(silu_step, 1)
            for i in range(20 + TILES):
                act.wait_ge(proj_done, i + 1)
                b0 = 2 * (i % 2)
                if i < 20:
                    n, c = divmod(i, 4)
                    if i == 12:
                        act.wait_ge(conv_step, 22)
                    dst = (Aq, Bk, Cy, Aq, Bk)[n][:, c, :].rearrange("p (a b) -> p a b", a=2)
                    src = bank(b0, 2).rearrange("p (a b) -> p a b", a=2)[:, :, 0:NT // 2]
                else:
                    b0 = 2 * ((i - 20) % 2)
                    dst, src = V[:, i - 20, :], bank(b0)
                if i // 4 == 3:
                    act.activation(dst[:, 0, 0:CTX], src[:, 0, 0:CTX], ACT.Copy)
                    lat = Aq[:, i % 4, CTX:NT].rearrange("p (j r c) -> p r j c", j=BLOCKS, r=ROWS)
                    early = (NT // 2 - CTX) // GRID_W
                    act.activation(lat[:, 0:early], src[:, 0, CTX:].rearrange("p (r j c) -> p r j c", j=BLOCKS, c=COL_BLOCK),
                                   ACT.Copy)
                    dst = lat[:, early:ROWS]
                    src = src[:, 1, :].rearrange("p (r j c) -> p r j c", j=BLOCKS, c=COL_BLOCK)
                act.activation(dst, src, ACT.Copy).then_inc(proj_out, 1)
            act.wait_ge(kt_done, 1)
            act.activation(KTOK, bank(4), ACT.Copy).then_inc(kt_out, 1)

            def scale(n):
                act.wait_ge(sc_done, n + 1)
                if n >= 3:
                    act.wait_ge(pt_done, n - 2)
                if UNITS[n][0] == "ctx":
                    dst, src = S[n % 3], bank(n % 2)
                else:
                    dst, src = S[n % 3][:, PAST:HALF], bank(6 + n % 2)[:, 0:PAST]
                act.activation(dst, src, ACT.Copy, scale=SCALE).then_inc(s_scaled, 1)

            def exponents(n):
                act.wait_ge(max_done, n + 1)
                parts = 4 if UNITS[n][0] == "ctx" else 1
                for i in range(parts):
                    v = S[n % 3][:, i * (HALF // parts):(i + 1) * (HALF // parts)]
                    act.activation(v, v, ACT.Exp, bias=NMAX[:, n % 3, i:i + 1], accum_out=RSUM[:, n % 3, i:i + 1]
                                   ).then_inc(exp_done, 1)

            def take_turned(n):
                act.wait_ge(pt_done, n + 1)
                if n >= 2:
                    act.wait_ge(pv_done, n - 1)
                act.activation(PT[n % 2], bank(2 + n % 2), ACT.Copy).then_inc(pt_out, 1)

            def take_out(n):
                kind, a, j, par = UNITS[n]
                if kind == "lat" and par == 0:
                    return
                act.wait_ge(pv_done, n + 1)
                src = bank(4 + out_block(n) % 2)
                if kind == "ctx":
                    own = slice(HD * a, HD * a + HD)
                    act.activation(YNA[own, :, 0:CTX], src[own].rearrange("p (a b) -> p a b", a=4),
                                   ACT.Copy).then_inc(po_out, 1)
                else:
                    dst = YNA[:, a, CTX:NT].rearrange("p (r c) -> p r c", c=GRID_W)[:, :, j * COL_BLOCK:(j + 1) * COL_BLOCK]
                    act.activation(dst, src[:, 0:P].rearrange("p (r c) -> p r c", c=COL_BLOCK), ACT.Copy
                                   ).then_inc(po_out, 1)

            for n in range(NU + 3):
                if n < NU:
                    scale(n)
                if 1 <= n <= NU:
                    exponents(n - 1)
                if 2 <= n <= NU + 1:
                    take_turned(n - 2)
                if n >= 3:
                    take_out(n - 3)

            for s, (t0, n_tok) in enumerate(SECTIONS):
                for i in range(8):
                    d = 8 * s + i
                    act.wait_ge(gates_done, d + 1)
                    if d >= 2:
                        act.wait_ge(merge_step, 2 * (d - 1))
                    if d == 8:
                        act.wait_ge(pick_step, PICKS)
                    src = bank(4 * (d % 2), 2).rearrange("p (a b) -> p a b", a=2)[:, :, 0:n_tok]
                    act.activation(SG[d % 2][:, :, 0:n_tok], src, ACT.Sigmoid).then_inc(sig_out, 1)
                tiles = (0,) if s == 0 else (1, 2, 3, 4)
                for e in tiles:
                    act.wait_ge(ln_step, LNS * e + 6)
                    act.activation(RSTD[:, 0:1], MV[:, 1:2], ACT.Sqrt).then_inc(sqrt_done, 1)
                    act.wait_ge(ut_done, e + 1)
                    act.activation(UT[:, :, e * P:(e + 1) * P], bank(4 + 2 * (e % 2), 2).rearrange("p (k t) -> p k t", t=P),
                                   ACT.Copy).then_inc(ut_out, 1)
                for f in range(16 * s, 16 * s + 16):
                    act.wait_ge(q_done, f + 1)
                    qg = f // 4
                    if qg >= 1:
                        act.wait_ge(ss_done, qg if s == 0 or qg == 4 else 4 + 4 * (qg - 4))
                    act.activation(QT[:, f % 4, 0:n_tok], bank(f % 2)[:, 0:n_tok], ACT.Copy).then_inc(q_out, 1)
                for e in tiles:
                    act.wait_ge(pick_step, PICKS * e + SUB_AT)
                    act.activation(SMAX, SMAX, ACT.Exp).then_inc(gexp_done, 1)

            for e in range(TILES):
                def groups(lo, hi):
                    with act.Fori(lo, hi) as g:
                        at_g = HK * e + GROUP * g
                        act.wait_ge(u_free, at_g + 2 * GROUP)
                        act.activation(GEL, DOT, ACT.Gelu).then_inc(gelu_done, 1)
                        act.wait_ge(w_ready, GROUPS * e + g + 1)
                        for b in range(GROUP):
                            act.wait_ge(v_free, at_g + (b + 1))
                            act.activation(DG[b], IDN, ACT.Copy, scale=WGT[:, b:b + 1]).then_inc(diag_ready, 1)

                groups(0, 2)
                if e >= 1:
                    act.wait_ge(fin_step, FIN * (e - 1) + 6)
                    act.activation(RSTD[:, 0:1], MV[:, 1:2], ACT.Sqrt).then_inc(fsqrt_done, 1)
                groups(2, GROUPS)
            act.wait_ge(fin_step, FIN * (TILES - 1) + 6)
            act.activation(RSTD[:, 0:1], MV[:, 1:2], ACT.Sqrt).then_inc(fsqrt_done, 1)

        @block.vector
        def _(dve):
            def layer_norm(step, base, out, gain, shift, sqrt_sem, sqrt_count):
                for hf in range(2):
                    dve.bn_stats(STAT[:, 6 * hf:6 * hf + 6], out[:, hf * HALF:(hf + 1) * HALF]).then_inc(step, 1)
                dve.wait_ge(step, base + 2)
                dve.bn_aggr(MV, STAT).then_inc(step, 1)
                dve.wait_ge(step, base + 3)
                dve.tensor_scalar(MV[:, 1:2], MV[:, 1:2], EPS, None, ALU.add).then_inc(step, 1)
                dve.wait_ge(sqrt_sem, sqrt_count)
                dve.reciprocal(RSTD[:, 1:2], RSTD[:, 0:1]).then_inc(step, 1)
                dve.wait_ge(step, base + 5)
                dve.tensor_scalar(out, out, MV[:, 0:1], RSTD[:, 1:2], ALU.subtract, ALU.mult).then_inc(step, 1)
                dve.wait_ge(step, base + 6)
                dve.tensor_tensor(out, out, gain, ALU.mult).then_inc(step, 1)
                dve.wait_ge(step, base + 7)
                dve.tensor_tensor(out, out, shift, ALU.add).then_inc(step, 1)

            dve.memset(ZERO, 0.0).then_inc(zero_set, 1)
            dve.wait_ge(silu_step, 1)
            dve.tensor_tensor(SIL, SIL, CT2, ALU.mult).then_inc(silu_step, 1)
            dve.wait_ge(bada_in, 16)

            def add_mods(g):
                dve.wait_ge(ada_done, g + 1)
                own = MODS[:, g * HALF:(g + 1) * HALF]
                dve.tensor_tensor(own, own, bank(6 + g % 2)[0:2, :], ALU.add).then_inc(mod_added, 1)

            for g in range(4):
                add_mods(g)
            dve.wait_ge(mod_added, 4)
            dve.tensor_scalar(MODS[:, D:2 * D], MODS[:, D:2 * D], 1.0, None, ALU.add).then_inc(mod_added, 1)
            dve.wait_ge(modt_done, 1)
            dve.tensor_copy(MODT, bank(5)[:, 0:32].rearrange("p (a b) -> p a b", b=2)).then_inc(modt_ready, 1)
            dve.wait_ge(modt_ready, 1)
            dve.wait_ge(x_in, 16 * KD)
            for k in range(KD):
                for s, (t0, n_tok) in enumerate(SECTIONS):
                    v = UT[:, k, t0:t0 + n_tok]
                    dve.tensor_scalar(v, v, MODT[:, KD + k, s:s + 1], MODT[:, k, s:s + 1], ALU.mult, ALU.add
                                      ).then_inc(u_ready, 1)
            for g in range(4, 10):
                add_mods(g)
            dve.wait_ge(proj_out, 12)
            dve.wait_ge(consts_in, 80)
            dve.tensor_tensor(Aq, Aq, Bk, ALU.mult).then_inc(conv_step, 1)
            dve.wait_ge(conv_step, 1)
            for c in range(4):
                dve.tensor_scalar(CT[:, c, :], Aq[:, c, :], CONVW[:, c, 1:2], None, ALU.mult).then_inc(conv_step, 1)
            dve.wait_ge(conv_step, 5)
            for c in range(4):
                for t0, n_tok in SECTIONS:
                    o = CT[:, c, t0 + 1:t0 + n_tok]
                    dve.scalar_tensor_tensor(o, Aq[:, c, t0:t0 + n_tok - 1], CONVW[:, c, 0:1], o, ALU.mult, ALU.add
                                             ).then_inc(conv_step, 1)
            dve.wait_ge(conv_step, 13)
            for c in range(4):
                for t0, n_tok in SECTIONS:
                    o = CT[:, c, t0:t0 + n_tok - 1]
                    dve.scalar_tensor_tensor(o, Aq[:, c, t0 + 1:t0 + n_tok], CONVW[:, c, 2:3], o, ALU.mult, ALU.add
                                             ).then_inc(conv_step, 1)
            dve.wait_ge(conv_step, 21)
            dve.tensor_tensor(Cy, Cy, CT, ALU.mult).then_inc(conv_step, 1)
            for g in range(10, 12):
                add_mods(g)
            dve.wait_ge(mod_added, 13)
            dve.tensor_scalar(MODS[:, 4 * D:5 * D], MODS[:, 4 * D:5 * D], 1.0, None, ALU.add).then_inc(mod_added, 1)

            def window(n):
                kind, a, j, par = UNITS[n]
                if kind == "lat":
                    if n == 2:
                        dve.wait_ge(bias_in, 16 * ROWS * HEADS)
                    dve.wait_ge(sc_done, n + 1)
                    if n >= 3:
                        dve.wait_ge(pt_done, n - 2)
                    h = 2 * a + par
                    off = BAND_START[j] - j * COL_BLOCK + COL_BLOCK
                    v = S[n % 3][:, 0:PAST].rearrange("p (r c) -> p r c", c=COL_BAND)
                    dve.scalar_tensor_tensor(v, bank(n % 2)[:, 0:PAST].rearrange("p (r c) -> p r c", c=COL_BAND), SCALE,
                                             WB[:, h, :, off:off + COL_BAND], ALU.mult, ALU.add).then_inc(win_step, 1)
                    dve.wait_ge(win_step, 2 * (n - 2) + 1)
                    mask = MASK[:, MASK_OF[j]:MASK_OF[j] + 1, :].to_broadcast([P, ROWS, COL_BAND])
                    dve.tensor_tensor(v, v, mask, ALU.add).then_inc(win_step, 1)
                    dve.wait_ge(win_step, 2 * (n - 1))
                dve.wait_ge(s_scaled, n + 1)
                parts = 4 if kind == "ctx" else 1
                dve.tensor_reduce(NMAX[:, n % 3, 0:parts], S[n % 3].rearrange("p (a b) -> p a b", a=parts), AX, ALU.max,
                                  negate=True).then_inc(max_done, 1)

            def normalise(n):
                parts = 4 if UNITS[n][0] == "ctx" else 1
                dve.wait_ge(exp_done, exps_upto(n))
                dve.reciprocal(RINV[:, n % 3, 0:parts], RSUM[:, n % 3, 0:parts]).then_inc(recip_done, 1)
                dve.wait_ge(recip_done, n + 1)
                for i in range(parts):
                    v = S[n % 3][:, i * (HALF // parts):(i + 1) * (HALF // parts)]
                    dve.tensor_scalar(v, v, RINV[:, n % 3, i:i + 1], None, ALU.mult).then_inc(norm_done, 1)

            for n in range(NU + 1):
                if n < NU:
                    window(n)
                if n >= 1:
                    normalise(n - 1)

            def route(e):
                base = PICKS * e
                val = VAL[:, e, :].rearrange("p (h s k) -> p h s k", s=2, k=TOPK)
                idxf = IDXF.rearrange("p (h s k) -> p h s k", s=2, k=TOPK)
                cube = [P, PEER_HEADS, TOPK, TOPK]
                dve.wait_ge(topk_step, 80 if e == 0 else 400)
                if e >= 1:
                    dve.wait_ge(pick_step, base)
                step = [base]

                def done(ins):
                    step[0] += 1
                    ins.then_inc(pick_step, 1)

                def settle():
                    dve.wait_ge(pick_step, step[0])

                cands = CANDS.rearrange("p h (a b) -> p h a b", b=TOPK)
                eq = EQ.rearrange("p h (a b) -> p h a b", b=TOPK)
                done(dve.tensor_tensor(cands, val[:, :, 0, :].unsqueeze(3).to_broadcast(cube),
                                       val[:, :, 1, :].unsqueeze(2).to_broadcast(cube), ALU.add))
                done(dve.tensor_copy(IDXF, IDXS[e]))
                settle()
                pos = POS.rearrange("p (h k) -> p h k", k=TOPK)
                for lo in (0, 8):
                    for h in range(PEER_HEADS):
                        done(dve.max(TOPS[:, h, lo:lo + 8], CANDS[:, h, :]))
                    settle()
                    for h in range(PEER_HEADS):
                        done(dve.max_index(pos[:, h, lo:lo + 8], TOPS[:, h, lo:lo + 8], CANDS[:, h, :]))
                    settle()
                    if lo == 0:
                        for h in range(PEER_HEADS):
                            done(dve.match_replace(CANDS[:, h, :], TOPS[:, h, 0:8], CANDS[:, h, :], LOWEST))
                        settle()
                smax = SMAX.rearrange("p (h k) -> p h k", k=TOPK)
                done(dve.tensor_tensor(smax, TOPS, TOPS[:, :, 0:1].to_broadcast([P, PEER_HEADS, TOPK]), ALU.subtract))
                assert step[0] == base + SUB_AT
                done(dve.tensor_scalar(PA, POS, 4, None, ALU.logical_shift_right))
                done(dve.tensor_scalar(PB, POS, TOPK - 1, None, ALU.bitwise_and))
                settle()
                done(dve.tensor_copy(AF, PA))
                done(dve.tensor_copy(BF, PB))
                settle()
                iota = IOTA.unsqueeze(1).unsqueeze(1).to_broadcast(cube)
                for side, digit, res in ((0, AF, I0), (1, BF, I1)):
                    d4 = digit.rearrange("p (h k) -> p h k", k=TOPK).unsqueeze(3).to_broadcast(cube)
                    done(dve.tensor_tensor(eq, d4, iota, ALU.is_equal))
                    settle()
                    done(dve.tensor_tensor(eq, eq, idxf[:, :, side, :].unsqueeze(2).to_broadcast(cube), ALU.mult))
                    settle()
                    done(dve.tensor_reduce(res.rearrange("p (h k) -> p h k", k=TOPK), eq, AX, ALU.add))
                    settle()
                done(dve.scalar_tensor_tensor(EID[:, e, :], I0, float(NKEYS), I1, ALU.mult, ALU.add))
                dve.wait_ge(gexp_done, e + 1)
                done(dve.tensor_reduce(GSUM, smax, AX, ALU.add))
                settle()
                done(dve.reciprocal(GSUM, GSUM))
                settle()
                done(dve.tensor_tensor(GATE[:, e, :].rearrange("p (h k) -> p h k", k=TOPK), smax,
                                       GSUM.unsqueeze(2).to_broadcast([P, PEER_HEADS, TOPK]), ALU.mult))
                assert step[0] == base + PICKS, step[0] - base

            IDXS = [IDX] + [at(33792 + 256 * i, 2 * PEER_HEADS * TOPK).bitcast(U32) for i in range(4)]

            for s, (t0, n_tok) in enumerate(SECTIONS):
                tiles = (0,) if s == 0 else (1, 2, 3, 4)
                for i in range(8):
                    d = 8 * s + i
                    sg = SG[d % 2][:, :, 0:n_tok]
                    dve.wait_ge(sig_out, d + 1)
                    dve.wait_ge(merge_done, d + 1)
                    dve.tensor_tensor(sg, sg, bank(4 * (d % 2) + 2, 2).rearrange("p (a b) -> p a b", a=2)[:, :, 0:n_tok],
                                      ALU.mult).then_inc(merge_step, 1)
                    dve.wait_ge(merge_step, 2 * d + 1)
                    dve.tensor_tensor(MT[:, i, 0:n_tok], sg[:, 0, :], sg[:, 1, :], ALU.add).then_inc(merge_step, 1)
                for e in tiles:
                    base = LNS * e
                    xr, xb, u2 = XR[e % 2], XB[e % 2], U2[e % 2]
                    dve.wait_ge(wo_done, e + 1)
                    dve.wait_ge(prm_in[s], 80 if s == 0 else 48)
                    if e >= 2:
                        dve.wait_ge(store_out[e % 2], 32 * (e // 2))
                    dve.tensor_tensor(xr, bank(2 * (e % 2), 2), PRM[0], ALU.mult).then_inc(ln_step, 1)
                    dve.wait_ge(ln_step, base + 1)
                    dve.wait_ge(xb_in[e % 2], 16 * (e // 2 + 1))
                    dve.scalar_tensor_tensor(xr, xb, ALPHA, xr, ALU.mult, ALU.add).then_inc(ln_step, 1)
                    dve.wait_ge(ln_step, base + 2)
                    layer_norm(ln_step, base + 2, xr, PRM[1], PRM[2], sqrt_done, e + 1)
                    dve.wait_ge(ln_step, base + 10)
                    dve.tensor_tensor(u2, xr, PRM[3], ALU.mult).then_inc(ln_step, 1)
                    dve.wait_ge(ln_step, base + 11)
                    dve.tensor_tensor(u2, u2, PRM[4], ALU.add).then_inc(ln_step, 1)
                for qg in range(4):
                    for tl, e in enumerate(tiles):
                        si = qg if s == 0 else 4 + 4 * qg + tl
                        idx = IDXS[e]
                        dve.wait_ge(ss_done, si + 1)
                        if si >= 1:
                            dve.wait_ge(topk_step, 20 * si)
                        sc = bank(2 + si % 2)
                        if e >= 1 and qg == 0 and tl == 0:
                            dve.wait_ge(ut_done, TILES)
                            all_stored(dve)

                        def best(c, lo):
                            o = (4 * qg + c) * TOPK + lo
                            return slice(o, o + 8)

                        for lo in (0, 8):
                            for c in range(4):
                                src = sc[:, c * P:(c + 1) * P] if lo == 0 else SW[:, c, :]
                                dve.max(VAL[:, e, best(c, lo)], src).then_inc(topk_step, 1)
                            dve.wait_ge(topk_step, 20 * si + 4 + 12 * (lo // 8))
                            for c in range(4):
                                src = sc[:, c * P:(c + 1) * P] if lo == 0 else SW[:, c, :]
                                dve.max_index(idx[:, best(c, lo)], VAL[:, e, best(c, lo)], src).then_inc(topk_step, 1)
                            if lo == 0:
                                for c in range(4):
                                    dve.match_replace(SW[:, c, :], VAL[:, e, best(c, 0)], sc[:, c * P:(c + 1) * P], LOWEST
                                                      ).then_inc(topk_step, 1)
                                dve.wait_ge(topk_step, 20 * si + 12)
                for e in tiles:
                    route(e)

            def finish(e):
                base = FIN * e
                yr = YR[e % 2]
                dve.wait_ge(y_done, e + 1)
                dve.wait_ge(prm2_in, 48 if e == 0 else 64)
                if e >= 2:
                    dve.wait_ge(y_out[e % 2], 16 * (e // 2))
                dve.tensor_tensor(yr, bank(4 + 2 * (e % 2), 2), PRM2[0], ALU.mult).then_inc(fin_step, 1)
                dve.wait_ge(fin_step, base + 1)
                dve.scalar_tensor_tensor(yr, X1B[e % 2], ALPHA, yr, ALU.mult, ALU.add).then_inc(fin_step, 1)
                dve.wait_ge(fin_step, base + 2)
                layer_norm(fin_step, base + 2, yr, PRM2[1], PRM2[2], fsqrt_done, e + 1)

            dve.wait_ge(pick_step, PICKS * TILES)
            dve.memset(DOT, 0.0).then_inc(u_free, GROUP)
            dve.wait_ge(u_free, GROUP)
            for e in range(TILES):
                dve.wait_ge(tile_in[e % 2], 32 * (e // 2 + 1))

                def groups(lo, hi):
                    with dve.Fori(lo, hi) as g:
                        for b in range(GROUP):
                            dve.wait_ge(u_land[b], 16 * GROUPS * e + 16 * g + 16)
                            dve.tensor_tensor_reduce(UR[b], UR[b], U2B[e % 2], 1.0, 0.0, ALU.mult, ALU.add,
                                                     DOT[:, b:b + 1]).then_inc(u_free, 1)
                        dve.wait_ge(gelu_done, GROUPS * e + g + 1)
                        dve.tensor_tensor(WGT, GEL, GATE[:, e, bass.ds(GROUP * g, GROUP)], ALU.mult).then_inc(w_ready, 1)

                groups(0, 2)
                if e >= 1:
                    finish(e - 1)
                groups(2, GROUPS)
            finish(TILES - 1)


LNS = 12
FIN = 10
SUB_AT = 2 + 5 * PEER_HEADS + 1
PICKS = SUB_AT + 4 + 6 + 4

_OUTS = [((1, CTX, D), "y_prompt"), ((1, LAT, D), "y_sample"), ((1, 1, CTX, HEADS, HD), "new_k"),
         ((1, 1, CTX, HEADS, HD), "new_v")]


def kernel(**inputs):
    import numpy as _np
    import concourse.bacc as _bacc
    from concourse import mybir as _mybir
    from concourse.bass_utils import run_bass_kernel_spmd as _run

    i = {k: _np.asarray(v) for k, v in inputs.items()}
    xs = _np.concatenate([i["x_prompt"][0], i["x_sample"][0]], axis=0)
    rpb = _np.pad(i["rpb"].reshape(-1), (16, 16))
    laid = {
        "x_prompt": i["x_prompt"], "x_sample": i["x_sample"], "xT": xs.T,
        "ck_T": i["cache_k"][0, 0].reshape(PAST, HEADS * HD).T, "cache_v": i["cache_v"],
        "c_T": _np.stack([i["c_ctx"], i["c"][0]], axis=-1).reshape(KD, P, 2).transpose(1, 0, 2),
        "w_ada": i["w_ada"], "b_ada": i["b_ada"], "w_in": i["w_in"],
        "convw_T": i["conv_w"][0].reshape(3, 4, P).transpose(2, 1, 0),
        "w_conv_out": i["w_conv_out"], "w_na_out": i["w_na_out"],
        "rpb_rows": _np.stack([rpb[15 - q:15 - q + rpb.size - 15] for q in range(COL_BLOCK)]),
        "w_o": i["w_o"], "ln1_g": i["ln1_g"], "ln1_b": i["ln1_b"], "w_query": i["w_query"],
        "sub_keys_T": i["sub_keys"][0].reshape(2 * PEER_HEADS, NKEYS, P).transpose(2, 0, 1),
        "expert_u": i["expert_u"], "expert_v": i["expert_v"], "ln2_g": i["ln2_g"], "ln2_b": i["ln2_b"],
        "ident_in": _np.eye(P, dtype=_np.float32), "mask_in": window_mask(),
        "iota_in": _np.tile(_np.arange(TOPK, dtype=_np.float32), (P, 1)),
    }
    nc = _bacc.Bacc("TRN2", target_bir_lowering=False, num_devices=1)
    arrays, args = {}, []
    for name, a in laid.items():
        a = _np.ascontiguousarray(a)
        arrays[f"in_{name}_dram"] = a
        args.append(nc.dram_tensor(f"in_{name}_dram", a.shape, _mybir.dt.from_np(a.dtype), kind="ExternalInput").ap())
    for shape, name in _OUTS:
        args.append(nc.dram_tensor(f"out_{name}_dram", shape, F32, kind="ExternalOutput").ap())
    backbone(nc, *args)
    r = _run(nc, [arrays], core_ids=[0])
    return tuple(r.results[0][f"out_{name}_dram"] for _, name in _OUTS)
```

```python
from contextlib import ExitStack

import numpy as np

import concourse.bass as bass
from concourse import mybir

ALU = mybir.AluOpType
ACT = mybir.ActivationFunctionType
AX = mybir.AxisListType.X
F32 = mybir.dt.float32
U32 = mybir.dt.uint32

P = 128
D = 1024
KD = D // P
CTX, LAT = 128, 512
NT = CTX + LAT
TILES = NT // P
SECTIONS = ((0, CTX), (CTX, LAT))
GRID_W, ROWS = 64, 8
PAST = 256
HEADS, HD = 8, 64
WIN_W, COL_BLOCK, COL_BAND = 16, 16, 32
WIDE = COL_BLOCK + COL_BAND
BLOCKS = GRID_W // COL_BLOCK
RPB_H, RPB_W = 15, 31
PEER_HEADS, TOPK, NKEYS = 8, 16, 128
HK = PEER_HEADS * TOPK
CAND = TOPK * TOPK
GROUP = 8
GROUPS = HK // GROUP
SCALE = HD ** -0.5
ALPHA = 2.0 ** 0.25
EPS = 1e-5
NEG = -1e30
LOWEST = -3.0e38
HALF = 512
WSLOTS = 3
QUAD = P // 4
LAG = 2

BAND_START = [min(max(j * COL_BLOCK - WIN_W // 2, 0), GRID_W - COL_BAND) for j in range(BLOCKS)]
MASK_OF = [0, 1, 1, 2]


def window_mask():
    m = np.zeros((P, 3, COL_BAND), np.float32)
    for j in (0, 1, 3):
        for p in range(P):
            q = j * COL_BLOCK + p % COL_BLOCK
            start = min(max(q - WIN_W // 2, 0), GRID_W - WIN_W)
            cols = BAND_START[j] + np.arange(COL_BAND)
            m[p, MASK_OF[j], (cols < start) | (cols >= start + WIN_W)] = NEG
    return m.reshape(P, 3 * COL_BAND)


def weight_loads():
    loads = [("ada", g) for g in range(4)]
    for n, g in enumerate(PROJ):
        loads.append(("in", g))
        if n < 4:
            loads += [("ada", 4 + 2 * n), ("ada", 5 + 2 * n)]
    loads.append(("in", 5))
    for s in range(2):
        for hf in range(2):
            loads += [("gconv", s, hf), ("gna", s, hf), ("branch", s, hf)]
        loads += [("out", s, 0), ("out", s, 1)]
        loads += [("query", s, g) for g in range(4)]
    return loads


PROJ = (0, 2, 1, 3, 4)


def mod_adds(g):
    return g + 1 if g < 4 else g + 2


def units():
    out = [("ctx", b, 0, 0) for b in range(2)]
    out += [("lat", hp, j, par) for hp in range(HEADS // 2) for j in range(BLOCKS) for par in range(2)]
    return out


UNITS = units()
NU = len(UNITS)


def exps_upto(n):
    return 4 * (n + 1) if n < 2 else 8 + (n - 1)


def outputs_upto(n):
    return n + 1 if n < 2 else 2 + (n - 1) // 2


def out_block(n):
    return n if n < 2 else 2 + (n - 2) // 2


def backbone(nc, x_prompt, x_sample, xT, ck_T, cache_v, c_T, w_ada, b_ada, w_in, convw_T, w_conv_out,
             w_na_out, rpb_rows, w_o, ln1_g, ln1_b, w_query, sub_keys_T, expert_u, expert_v, ln2_g, ln2_b,
             ident_in, mask_in, iota_in, pickrow_in,
             y_prompt, y_sample, new_k, new_v):
    mods_d = nc.dram_tensor("mods_d", (2, 6 * D), F32, kind="Internal").ap()
    x1_d = nc.dram_tensor("x1_d", (NT, D), F32, kind="Internal").ap()
    u2_d = nc.dram_tensor("u2_d", (NT, D), F32, kind="Internal").ap()

    def rows(prompt, sample, e):
        return prompt[0] if e == 0 else sample[0, (e - 1) * P:e * P, :]

    with ExitStack() as ctx:
        def sem(name):
            return ctx.enter_context(nc.semaphore(name))

        arena = ctx.enter_context(nc.sbuf_tensor("arena", [P, 53184], F32))
        psum = ctx.enter_context(nc.psum_tensor("psum", [P, 8 * HALF], F32))

        def bank(b, n=1):
            return psum[:, b * HALF:(b + n) * HALF]

        def at(off, *shape):
            n = int(np.prod(shape))
            v = arena[:, off:off + n]
            if len(shape) == 2:
                v = v.rearrange("p (a b) -> p a b", b=shape[1])
            if len(shape) == 3:
                v = v.rearrange("p (a b c) -> p a b c", b=shape[1], c=shape[2])
            return v

        W = [at(4096 * i, KD, HALF) for i in range(WSLOTS)]
        UT = at(12288, KD, NT)
        Aq, Bk, Cy = at(17408, 4, NT), at(19968, 4, NT), at(22528, 4, NT)
        MT = at(17408, KD, LAT)
        V = at(25088, TILES, HALF)
        VB = at(27648, 2 * BLOCKS, HALF)
        MODS = at(27648, 6 * D)[0:2, :]
        SG = [at(27648 + 1024 * i, 2, HALF) for i in range(2)]
        XB = [at(29696 + 1024 * i, D) for i in range(2)]
        CK = at(31744, 4, PAST)
        CV = at(32768, 2, HALF)
        XR = [at(31744 + 1024 * i, D) for i in range(2)]
        WB = at(33792, HEADS, ROWS, WIDE)
        U2 = [at(33792 + 1024 * i, D) for i in range(2)]
        YNA = at(36864, 4, NT)
        CT = at(36864, 4, NT)
        S = [at(39424 + HALF * i, HALF) for i in range(3)]
        PT = [at(40960 + HALF * i, HALF) for i in range(2)]
        PRM = [at(o, D) for o in (25088, 26112, 39424, 40448, 35840)]
        SK = at(41984, 2 * PEER_HEADS, NKEYS)
        QT = at(44032, 4, LAT)
        CANDS = at(27648, PEER_HEADS, CAND)
        EQ = at(29696, PEER_HEADS, CAND)
        IDN = at(46080, P)
        ZERO = at(46208, HALF)
        VAL = at(46720, TILES, 2 * PEER_HEADS * TOPK)
        IDX = at(48000, 2 * PEER_HEADS * TOPK).bitcast(U32)
        IDXF = at(48256, 2 * PEER_HEADS * TOPK)
        EID = at(48512, TILES, HK).bitcast(U32)
        GATE = at(49152, TILES, HK)
        MODT = at(49792, 16, 2)
        CONVW = at(49824, 4, 3)
        MASK = at(49836, 3, COL_BAND)
        IOTA = at(49932, TOPK)
        CT2 = at(49948, KD, 2)
        SIL = at(49964, KD, 2)
        NMAX = at(49980, 3, 4)
        RSUM = at(49992, 3, 4)
        RINV = at(50004, 3, 4)
        STAT = at(50016, 12)
        MV = at(50028, 2)
        RSTD = at(50030, 2)
        SMAX = at(50032, HK)
        AF = at(50160, HK)
        BF = at(50288, HK)
        POS = at(50416, HK).bitcast(U32)
        TOPS = at(50544, PEER_HEADS, TOPK)
        GSUM = at(50672, PEER_HEADS)
        DOT = at(50680, GROUP)
        NUM = [at(50688 + GROUP * i, GROUP).bitcast(U32) for i in range(2)]
        PA = at(50712, HK).bitcast(U32)
        PB = at(50840, HK).bitcast(U32)
        SW = at(50968, 4, NKEYS)
        KTOK = at(51480, HALF)
        I0 = at(51992, HK)
        I1 = at(52120, HK)
        UR = [at(1024 * i, D) for i in range(GROUP)]
        VR = [at(8192 + 1024 * i, D) for i in range(GROUP)]
        EIDT = [at(16384 + P * i, P).bitcast(U32) for i in range(2)]
        WT = [at(16640 + P * i, P) for i in range(2)]
        WTOK = at(16896, HK)
        U2B = [at(17408 + 1024 * i, D) for i in range(2)]
        X1B = [at(19456 + 1024 * i, D) for i in range(2)]
        PRM2 = [at(21504 + 1024 * i, D) for i in range(3)]
        DOTS = [at(27136 + HK * i, HK) for i in range(2)]
        WCOL = [at(27392, 4, QUAD), at(27520, 4, QUAD)]
        PICKROW = at(35840, QUAD, QUAD)
        EIDF = [at(52248 + HK * i, HK) for i in range(2)]
        YR = [at(25088 + 1024 * i, D) for i in range(2)]

        w_land = [sem(f"w_land{i}") for i in range(WSLOTS)]
        consts_in, x_in, bias_in, ctx_in = sem("consts_in"), sem("x_in"), sem("bias_in"), sem("ctx_in")
        bada_in, keys_in = sem("bada_in"), sem("keys_in")
        silu_step, ada_done, mod_added, modt_done, modt_ready = (
            sem("silu_step"), sem("ada_done"), sem("mod_added"), sem("modt_done"), sem("modt_ready"))
        u_ready, mods_out = sem("u_ready"), sem("mods_out")
        proj_done, proj_out, conv_step = sem("proj_done"), sem("proj_out"), sem("conv_step")
        kt_done, kt_out, cache_out, band_in = sem("kt_done"), sem("kt_out"), sem("cache_out"), sem("band_in")
        sc_done, s_scaled, win_step, max_done, exp_done = (
            sem("sc_done"), sem("s_scaled"), sem("win_step"), sem("max_done"), sem("exp_done"))
        recip_done, norm_done, pt_done, pt_out, pv_done, po_out = (
            sem("recip_done"), sem("norm_done"), sem("pt_done"), sem("pt_out"), sem("pv_done"), sem("po_out"))
        gates_done, merge_done, sig_out, merge_step = (
            sem("gates_done"), sem("merge_done"), sem("sig_out"), sem("merge_step"))
        prm_in = [sem("prm_in0"), sem("prm_in1")]
        xb_in = [sem("xb_in0"), sem("xb_in1")]
        store_out = [sem("store_out0"), sem("store_out1")]
        wo_done, ln_step, sqrt_done, ut_done, ut_out = (
            sem("wo_done"), sem("ln_step"), sem("sqrt_done"), sem("ut_done"), sem("ut_out"))
        q_done, q_out, ss_done, topk_step, pick_step, gexp_done = (
            sem("q_done"), sem("q_out"), sem("ss_done"), sem("topk_step"), sem("pick_step"), sem("gexp_done"))
        x1_in, u2_in = [sem("x1_in0"), sem("x1_in1")], [sem("u2_in0"), sem("u2_in1")]
        prm2_in, u_land, v_land = sem("prm2_in"), [sem(f"u_land{i}") for i in range(GROUP)], [
            sem(f"v_land{i}") for i in range(GROUP)]
        num_ready, u_free, v_free, dots_out, cols_ready = (
            sem("num_ready"), sem("u_free"), sem("v_free"), sem("dots_out"), sem("cols_ready"))
        gelu_done, weighed, rank_done, rank_out = sem("gelu_done"), sem("weighed"), sem("rank_done"), sem("rank_out")
        zero_set, y_done, fin_step, fsqrt_done = (
            sem("zero_set"), sem("y_done"), sem("fin_step"), sem("fsqrt_done"))
        y_out = [sem("y_out0"), sem("y_out1")]
        pick_in = sem("pick_in")

        loads = weight_loads()
        slot_of = {key: n % WSLOTS for n, key in enumerate(loads)}
        counts, landed = [0] * WSLOTS, {}
        for n, key in enumerate(loads):
            counts[n % WSLOTS] += 32 if key[0] == "branch" else 16
            landed[key] = counts[n % WSLOTS]

        def freed_by(key):
            kind = key[0]
            if kind == "ada":
                return ada_done, key[1] + 1
            if kind == "in":
                return proj_done, 4 * (PROJ.index(key[1]) + 1) if key[1] != 5 else 20 + TILES
            if kind in ("gconv", "gna", "branch"):
                return merge_done, 8 * key[1] + 4 * key[2] + 4
            if kind == "out":
                return wo_done, 1 if key[1] == 0 else TILES
            return q_done, 16 * key[1] + 4 * key[2] + 4

        def weights(pe, key):
            pe.wait_ge(w_land[slot_of[key]], landed[key])
            return W[slot_of[key]]

        def w_cols(w, c0, n=HALF):
            return w[:, c0:c0 + n].rearrange("(k p) n -> p k n", p=P)

        def all_stored(eng):
            for i in range(2):
                eng.wait_ge(store_out[i], 32 * len(range(i, TILES, 2)))

        block = ctx.enter_context(nc.Block())

        @block.sync
        def _(sp):
            for n, key in enumerate(loads):
                if n >= WSLOTS:
                    sp.wait_ge(*freed_by(loads[n - WSLOTS]))
                dst, done = W[n % WSLOTS], w_land[n % WSLOTS]
                kind = key[0]
                if kind == "ada":
                    sp.dma_start(dst, w_cols(w_ada[0], key[1] * HALF)).then_inc(done, 16)
                elif kind == "in":
                    sp.dma_start(dst, w_cols(w_in[0], key[1] * HALF)).then_inc(done, 16)
                elif kind == "gconv":
                    sp.dma_start(dst, w_cols(w_in[0], (6 + key[2]) * HALF)).then_inc(done, 16)
                elif kind == "gna":
                    sp.dma_start(dst, w_cols(w_in[0], (8 + key[2]) * HALF)).then_inc(done, 16)
                elif kind == "branch":
                    sp.dma_start(dst[:, 0:4, :], w_cols(w_conv_out[0], key[2] * HALF)).then_inc(done, 16)
                    sp.dma_start(dst[:, 4:8, :], w_cols(w_na_out[0], key[2] * HALF)).then_inc(done, 16)
                elif kind == "out":
                    sp.dma_start(dst, w_cols(w_o[0], key[2] * HALF)).then_inc(done, 16)
                else:
                    sp.dma_start(dst, w_cols(w_query[0], key[2] * HALF)).then_inc(done, 16)

            def load_u2(e):
                if e >= 2:
                    sp.wait_ge(u_free, HK * (e - 1) + GROUP)
                sp.dma_start(U2B[e % 2], u2_d[e * P:(e + 1) * P, :]).then_inc(u2_in[e % 2], 16)

            def load_x1(e):
                if e >= 2:
                    sp.wait_ge(fin_step, FIN * (e - 1))
                sp.dma_start(X1B[e % 2], x1_d[e * P:(e + 1) * P, :]).then_inc(x1_in[e % 2], 16)

            def second_gate(s):
                sp.dma_start(PRM2[0], mods_d[s:s + 1, 5 * D:6 * D].partition_broadcast(P)).then_inc(prm2_in, 16)

            def store_y(e):
                sp.wait_ge(fin_step, FIN * (e + 1))
                sp.dma_start(rows(y_prompt, y_sample, e), YR[e % 2]).then_inc(y_out[e % 2], 16)

            sp.wait_ge(q_done, 32)
            all_stored(sp)
            load_u2(0)
            sp.dma_start(PICKROW, pickrow_in.partition_broadcast(P)).then_inc(pick_in, 16)
            load_u2(1)
            load_x1(0)
            load_x1(1)
            sp.dma_start(PRM2[1], ln2_g[0:1, :].partition_broadcast(P)).then_inc(prm2_in, 16)
            sp.dma_start(PRM2[2], ln2_b[0:1, :].partition_broadcast(P)).then_inc(prm2_in, 16)
            second_gate(0)
            load_u2(2)
            load_u2(3)
            store_y(0)
            second_gate(1)
            load_x1(2)
            load_u2(4)
            for e in range(1, TILES):
                store_y(e)
                if e + 2 < TILES:
                    load_x1(e + 2)
            for i in range(2):
                sp.wait_ge(y_out[i], 16 * len(range(i, TILES, 2)))
            sp.wait_ge(cache_out, 32)

        def store_tile(pool, e):
            pool.wait_ge(ln_step, LNS * (e + 1))
            pool.dma_start(x1_d[e * P:(e + 1) * P, :], XR[e % 2]).then_inc(store_out[e % 2], 16)
            pool.dma_start(u2_d[e * P:(e + 1) * P, :], U2[e % 2]).then_inc(store_out[e % 2], 16)

        @block.gpsimd
        def _(pool):
            pool.dma_start(CT2, c_T).then_inc(consts_in, 16)
            pool.dma_start(IDN, ident_in).then_inc(consts_in, 16)
            pool.dma_start(MODS, b_ada[0:1, :].partition_broadcast(2)).then_inc(bada_in, 16)
            for k in range(KD):
                pool.dma_start(UT[:, k, :], xT[k * P:(k + 1) * P, :]).then_inc(x_in, 16)
            pool.dma_start(CONVW, convw_T).then_inc(consts_in, 16)
            pool.dma_start(MASK, mask_in.rearrange("p (a b) -> p a b", b=COL_BAND)).then_inc(consts_in, 16)
            pool.dma_start(IOTA, iota_in).then_inc(consts_in, 16)
            pool.dma_start(SK, sub_keys_T).then_inc(keys_in, 16)
            length = rpb_rows.shape[1]
            for r in range(ROWS):
                for h in range(HEADS):
                    src = bass.AP(rpb_rows.tensor, h * RPB_H * RPB_W + (ROWS - 1 - r) * RPB_W,
                                  [[length, COL_BLOCK], [RPB_W, ROWS], [1, WIDE]])
                    pool.dma_start(WB[r * COL_BLOCK:(r + 1) * COL_BLOCK, h], src).then_inc(bias_in, 16)
            pool.wait_ge(mod_added, 14)
            pool.dma_start(mods_d, MODS).then_inc(mods_out, 16)
            pool.wait_ge(mods_out, 16)
            for t in range(2):
                pool.dma_start(CV[:, t, :], cache_v[0, 0, t * P:(t + 1) * P].rearrange("t h d -> t (h d)")
                               ).then_inc(ctx_in, 16)
            for c in range(4):
                pool.dma_start(CK[:, c, :], ck_T[c * P:(c + 1) * P, :]).then_inc(ctx_in, 16)
            pool.wait_ge(proj_out, 20 + TILES)
            for j in range(BLOCKS):
                for i in range(ROWS):
                    p0 = (i % 2) * GRID_W + BAND_START[j]
                    pool.dma_start(VB[(i % 4) * COL_BAND:(i % 4 + 1) * COL_BAND, 2 * j + i // 4, :],
                                   V[p0:p0 + COL_BAND, 1 + i // 2, :]).then_inc(band_in, 16)
            pool.dma_start(new_v[0, 0].rearrange("t h d -> t (h d)"), V[:, 0, :]).then_inc(cache_out, 16)
            pool.wait_ge(kt_out, 1)
            pool.dma_start(new_k[0, 0].rearrange("t h d -> t (h d)"), KTOK).then_inc(cache_out, 16)

            pool.wait_ge(po_out, outputs_upto(NU - 1))
            pool.wait_ge(band_in, 16 * BLOCKS * ROWS)
            pool.wait_ge(cache_out, 32)
            for s in range(2):
                if s == 1:
                    pool.wait_ge(ln_step, LNS)
                pool.dma_start(PRM[0], mods_d[s:s + 1, 2 * D:3 * D].partition_broadcast(P)).then_inc(prm_in[s], 16)
                pool.dma_start(PRM[4], mods_d[s:s + 1, 3 * D:4 * D].partition_broadcast(P)).then_inc(prm_in[s], 16)
                pool.dma_start(PRM[3], mods_d[s:s + 1, 4 * D:5 * D].partition_broadcast(P)).then_inc(prm_in[s], 16)
                if s == 0:
                    pool.dma_start(PRM[1], ln1_g[0:1, :].partition_broadcast(P)).then_inc(prm_in[s], 16)
                    pool.dma_start(PRM[2], ln1_b[0:1, :].partition_broadcast(P)).then_inc(prm_in[s], 16)
                else:
                    pool.wait_ge(pick_step, PICKS)
                for e in ((0,) if s == 0 else (1, 2, 3, 4)):
                    if e >= 3:
                        pool.wait_ge(ln_step, LNS * (e - 1))
                    pool.dma_start(XB[e % 2], rows(x_prompt, x_sample, e)).then_inc(xb_in[e % 2], 16)
                    if e >= 2:
                        store_tile(pool, e - 1)
                store_tile(pool, 0 if s == 0 else TILES - 1)

            pool.wait_ge(q_out, 32)
            all_stored(pool)

            def numbers(side, table, b0, source):
                own = slice(b0, b0 + 4)
                pool.tensor_copy(NUM[side][:, own], source).then_inc(num_ready, 1)
                pool.wait_ge(num_ready, 1)
                pool.sem_clear(num_ready)
                for b in range(b0, b0 + 4):
                    slot, land = ((UR[b], u_land[b]), (VR[b], v_land[b]))[side]
                    pool.indirect_dma_start(slot, None, table[0], bass.IndirectOffsetOnAxis(
                        ap=NUM[side][:, b:b + 1], axis=0)).then_inc(land, 16)

            def stretch(n, u=None, v=None):
                with pool.Fori(0, n) as g:
                    for b0 in (0, 4):
                        if u:
                            e, g0 = u
                            pool.wait_ge(u_free, GROUP * g + (HK * e + GROUP * g0 + b0 + 4))
                            numbers(0, expert_u, b0, EID[:, e, bass.ds(GROUP * g + (GROUP * g0 + b0), 4)])
                        if v:
                            e, g0 = v
                            pool.wait_ge(v_free, GROUP * g + (HK * e + GROUP * g0 + b0 + 4))
                            numbers(1, expert_v, b0, EIDT[e % 2][:, bass.ds(GROUP * g + (GROUP * g0 + b0), 4)])
                            w = WT[e % 2][:, bass.ds(GROUP * g + (GROUP * g0 + b0), 4)]
                            row = PICKROW[:, bass.ds(2 * g + (2 * g0 + b0 // 4), 1), :]
                            pool.tensor_tensor(WCOL[b0 // 4], w.unsqueeze(2).to_broadcast([P, 4, QUAD]),
                                               row.to_broadcast([P, 4, QUAD]), ALU.mult).then_inc(cols_ready, 1)

            def routed(e):
                pool.wait_ge(pick_step, PICKS * (e + 1))

            stretch(GROUPS, u=(0, 0))
            routed(1)
            stretch(LAG, u=(1, 0))
            pool.wait_ge(pick_in, 16)
            for e in range(TILES):
                pool.wait_ge(rank_out, 2 * (e + 1))
                more = e + 1 < TILES
                stretch(GROUPS - LAG, u=(e + 1, LAG) if more else None, v=(e, 0))
                more = e + 2 < TILES
                if more:
                    routed(e + 2)
                stretch(LAG, u=(e + 2, 0) if more else None, v=(e, GROUPS - LAG))

        @block.tensor
        def _(pe):
            def ada(g):
                w = weights(pe, ("ada", g))
                if g >= 2:
                    pe.wait_ge(mod_added, mod_adds(g - 2))
                for k in range(KD):
                    mm = pe.matmul(bank(6 + g % 2)[0:2, :], SIL[:, k, :], w[:, k, :], start=k == 0, stop=k == KD - 1)
                mm.then_inc(ada_done, 1)

            def project(n):
                w = weights(pe, ("in", PROJ[n]))
                for c in range(4):
                    i = 4 * n + c
                    if i >= 2:
                        pe.wait_ge(proj_out, i - 1)
                    for k in range(KD):
                        for hf in range(2):
                            mm = pe.matmul(bank(2 * (i % 2) + hf)[:, 0:NT // 2], w[:, k, c * P:(c + 1) * P],
                                           UT[:, k, hf * (NT // 2):(hf + 1) * (NT // 2)],
                                           start=k == 0, stop=k == KD - 1)
                    mm.then_inc(proj_done, 1)

            pe.wait_ge(silu_step, 2)
            for g in range(4):
                ada(g)
            pe.wait_ge(mod_added, 5)
            pe.wait_ge(consts_in, 80)
            for m in range(16):
                mm = pe.transpose(bank(5)[:, 2 * m:2 * m + 2], MODS[:, m * P:(m + 1) * P], IDN[0:2, 0:2])
            mm.then_inc(modt_done, 1)
            pe.wait_ge(u_ready, 16)
            for n in range(5):
                project(n)
                if n < 4:
                    ada(4 + 2 * n)
                    ada(5 + 2 * n)
            w = weights(pe, ("in", 5))
            for t in range(TILES):
                pe.wait_ge(proj_out, 20 + t - 1)
                for k in range(KD):
                    mm = pe.matmul(bank(2 * (t % 2)), UT[:, k, t * P:(t + 1) * P], w[:, k, :], start=k == 0,
                                   stop=k == KD - 1)
                mm.then_inc(proj_done, 1)
            for c in range(4):
                mm = pe.transpose(bank(4)[:, c * P:(c + 1) * P], Bk[:, c, 0:CTX], IDN)
            mm.then_inc(kt_done, 1)

            def scores(n):
                kind, a, j, par = UNITS[n]
                out = bank(n % 2)
                if n == 0:
                    pe.wait_ge(proj_out, 20 + TILES)
                if n >= 2:
                    pe.wait_ge(s_scaled, n - 1)
                if n >= 4:
                    pe.wait_ge(win_step, 2 * (n - 3))
                if kind == "ctx":
                    for i in range(4):
                        p = slice(HD * a, HD * a + HD)
                        mm = pe.matmul(out[:, i * P:(i + 1) * P], Aq[p, i, 0:CTX], Bk[p, i, 0:CTX],
                                       start=True, stop=True)
                else:
                    if n == 2:
                        pe.wait_ge(ctx_in, 96)
                    p = slice(HD * par, HD * par + HD)
                    q = Aq[p, a, CTX + j * P:CTX + (j + 1) * P]
                    k = Bk[p, a, CTX:NT].rearrange("p (r c) -> p r c", c=GRID_W)[:, :, BAND_START[j]:BAND_START[j] + COL_BAND]
                    pe.matmul(out[:, 0:PAST].rearrange("p (r c) -> p r c", c=COL_BAND), q, k, start=True, stop=True)
                    mm = pe.matmul(bank(6 + n % 2)[:, 0:PAST], q, CK[p, a, :], start=True, stop=True)
                mm.then_inc(sc_done, 1)

            def turn(n):
                pe.wait_ge(norm_done, exps_upto(n))
                if n >= 2:
                    pe.wait_ge(pt_out, n - 1)
                for i in range(4):
                    mm = pe.transpose(bank(2 + n % 2)[:, i * P:(i + 1) * P], S[n % 3][:, i * P:(i + 1) * P], IDN)
                mm.then_inc(pt_done, 1)

            def mix(n):
                kind, a, j, par = UNITS[n]
                o = out_block(n)
                pe.wait_ge(pt_out, n + 1)
                if o >= 2:
                    pe.wait_ge(po_out, o - 1)
                if n == 0:
                    pe.wait_ge(kt_out, 1)
                out = bank(4 + o % 2)
                if kind == "ctx":
                    for i in range(4):
                        h = 2 * i + a
                        mm = pe.matmul(out[HD * a:HD * a + HD, i * P:(i + 1) * P],
                                       V[:, 0, h * HD:(h + 1) * HD], PT[n % 2][:, i * P:(i + 1) * P],
                                       start=True, stop=True)
                else:
                    if n == 2:
                        pe.wait_ge(band_in, 16 * BLOCKS * ROWS)
                    h = 2 * a + par
                    for i in range(4):
                        v = VB[:, 2 * j + i, h * HD:(h + 1) * HD] if i < 2 else CV[:, i - 2, h * HD:(h + 1) * HD]
                        mm = pe.matmul(out[HD * par:HD * par + HD, 0:P], v, PT[n % 2][:, i * P:(i + 1) * P],
                                       start=i == 0, stop=i == 3)
                mm.then_inc(pv_done, 1)

            for n in range(NU + 2):
                if n < NU:
                    scores(n)
                if 1 <= n <= NU:
                    turn(n - 1)
                if n >= 2:
                    mix(n - 2)

            pe.wait_ge(po_out, outputs_upto(NU - 1))
            for s, (t0, n_tok) in enumerate(SECTIONS):
                tok = slice(t0, t0 + n_tok)
                if s == 1:
                    pe.wait_ge(topk_step, 80)
                for hf in range(2):
                    wc, wn, wb = (weights(pe, (kind, s, hf)) for kind in ("gconv", "gna", "branch"))
                    for c in range(4):
                        d = 8 * s + 4 * hf + c
                        if 8 * s + 4 * hf + c >= 2:
                            pe.wait_ge(merge_step, 2 * (d - 1))
                        col = slice(c * P, (c + 1) * P)
                        b0 = 4 * (d % 2)
                        for k in range(KD):
                            pe.matmul(bank(b0)[:, 0:n_tok], wc[:, k, col], UT[:, k, tok], start=k == 0, stop=k == KD - 1)
                        for k in range(KD):
                            mm = pe.matmul(bank(b0 + 1)[:, 0:n_tok], wn[:, k, col], UT[:, k, tok], start=k == 0,
                                           stop=k == KD - 1)
                        mm.then_inc(gates_done, 1)
                        for k in range(4):
                            pe.matmul(bank(b0 + 2)[:, 0:n_tok], wb[:, k, col], Cy[:, k, tok], start=k == 0, stop=k == 3)
                        for k in range(4):
                            mm = pe.matmul(bank(b0 + 3)[:, 0:n_tok], wb[:, 4 + k, col], YNA[:, k, tok], start=k == 0,
                                           stop=k == 3)
                        mm.then_inc(merge_done, 1)
                pe.wait_ge(merge_step, 16 * (s + 1))
                w0, w1 = weights(pe, ("out", s, 0)), weights(pe, ("out", s, 1))
                tiles = (0,) if s == 0 else (1, 2, 3, 4)

                def turn_u2(e):
                    pe.wait_ge(ln_step, LNS * (e + 1))
                    if e >= 2:
                        pe.wait_ge(ut_out, e - 1)
                    for k in range(KD):
                        mm = pe.transpose(bank(4 + 2 * (e % 2), 2)[:, k * P:(k + 1) * P],
                                          U2[e % 2][:, k * P:(k + 1) * P], IDN)
                    mm.then_inc(ut_done, 1)

                for e in tiles:
                    loc = slice((e - tiles[0]) * P, (e - tiles[0] + 1) * P)
                    if e >= 3:
                        pe.wait_ge(ln_step, LNS * (e - 2) + 1)
                    for hf, w in enumerate((w0, w1)):
                        for k in range(KD):
                            mm = pe.matmul(bank(2 * (e % 2) + hf), MT[:, k, loc], w[:, k, :], start=k == 0,
                                           stop=k == KD - 1)
                    mm.then_inc(wo_done, 1)
                    if e > tiles[0]:
                        turn_u2(e - 1)
                turn_u2(tiles[-1])
                pe.wait_ge(ut_out, tiles[-1] + 1)
                pe.wait_ge(keys_in, 16)
                for qg in range(4):
                    w = weights(pe, ("query", s, qg))
                    for c in range(4):
                        f = 16 * s + 4 * qg + c
                        if f >= 2:
                            pe.wait_ge(q_out, f - 1)
                        for k in range(KD):
                            mm = pe.matmul(bank(f % 2)[:, 0:n_tok], w[:, k, c * P:(c + 1) * P], UT[:, k, tok],
                                           start=k == 0, stop=k == KD - 1)
                        mm.then_inc(q_done, 1)
                    pe.wait_ge(q_out, 16 * s + 4 * qg + 4)
                    for tl in range(len(tiles)):
                        si = qg if s == 0 else 4 + 4 * qg + tl
                        if si >= 2:
                            pe.wait_ge(topk_step, 20 * (si - 1))
                        for c in range(4):
                            mm = pe.matmul(bank(2 + si % 2)[:, c * P:(c + 1) * P], QT[:, c, tl * P:(tl + 1) * P],
                                           SK[:, 4 * qg + c, :], start=True, stop=True)
                        mm.then_inc(ss_done, 1)

            def rank(e):
                pe.wait_ge(pick_step, PICKS * (e + 1))
                if e >= 1:
                    pe.wait_ge(rank_out, 2 * e)
                pe.transpose(bank(2)[:, 0:P], EIDF[e % 2], IDN).then_inc(rank_done, 1)
                pe.wait_ge(weighed, e + 1)
                pe.transpose(bank(3)[:, 0:P], WTOK, IDN).then_inc(rank_done, 1)

            pe.wait_ge(zero_set, 1)
            pe.wait_ge(topk_step, 400)
            rank(0)
            for e in range(TILES):
                y = bank(4 + 2 * (e % 2), 2)
                if e >= 2:
                    pe.wait_ge(fin_step, FIN * (e - 2) + 1)
                for hf in range(2):
                    mm = pe.matmul(y[:, hf * HALF:(hf + 1) * HALF], ZERO[:, 0:P], ZERO, start=True, stop=False)
                if e == 0:
                    mm.then_inc(v_free, GROUP)

                def groups(lo, hi):
                    with pe.Fori(lo, hi) as g:
                        for b0 in (0, 4):
                            pe.wait_ge(cols_ready, 2 * g + (2 * GROUPS * e + b0 // 4 + 1))
                            for j in range(4):
                                pe.wait_ge(v_land[b0 + j], 16 * GROUPS * e + 16 * g + 16)
                            for hf in range(2):
                                for j in range(4):
                                    mm = pe.matmul(y[QUAD * j:QUAD * (j + 1), hf * HALF:(hf + 1) * HALF],
                                                   WCOL[b0 // 4][:, j, :], VR[b0 + j][:, hf * HALF:(hf + 1) * HALF],
                                                   start=False, stop=False, tile_position=(0, QUAD * j))
                            mm.then_inc(v_free, 4)

                groups(0, GROUPS - 1)
                if e + 1 < TILES:
                    rank(e + 1)
                groups(GROUPS - 1, GROUPS)
                for hf in range(2):
                    mm = pe.matmul(y[:, hf * HALF:(hf + 1) * HALF], ZERO[:, 0:P], ZERO, start=False, stop=True)
                mm.then_inc(y_done, 1)

        @block.scalar
        def _(act):
            act.wait_ge(consts_in, 80)
            act.activation(SIL, CT2, ACT.Sigmoid).then_inc(silu_step, 1)
            for i in range(20 + TILES):
                act.wait_ge(proj_done, i + 1)
                b0 = 2 * (i % 2)
                if i < 20:
                    n, c = divmod(i, 4)
                    if i == 12:
                        act.wait_ge(conv_step, 22)
                    dst = (Aq, Bk, Cy, Aq, Bk)[n][:, c, :].rearrange("p (a b) -> p a b", a=2)
                    src = bank(b0, 2).rearrange("p (a b) -> p a b", a=2)[:, :, 0:NT // 2]
                else:
                    b0 = 2 * ((i - 20) % 2)
                    dst, src = V[:, i - 20, :], bank(b0)
                if i // 4 == 3:
                    act.activation(dst[:, 0, 0:CTX], src[:, 0, 0:CTX], ACT.Copy)
                    lat = Aq[:, i % 4, CTX:NT].rearrange("p (j r c) -> p r j c", j=BLOCKS, r=ROWS)
                    early = (NT // 2 - CTX) // GRID_W
                    act.activation(lat[:, 0:early], src[:, 0, CTX:].rearrange("p (r j c) -> p r j c", j=BLOCKS, c=COL_BLOCK),
                                   ACT.Copy)
                    dst = lat[:, early:ROWS]
                    src = src[:, 1, :].rearrange("p (r j c) -> p r j c", j=BLOCKS, c=COL_BLOCK)
                act.activation(dst, src, ACT.Copy).then_inc(proj_out, 1)
            act.wait_ge(kt_done, 1)
            act.activation(KTOK, bank(4), ACT.Copy).then_inc(kt_out, 1)

            def scale(n):
                act.wait_ge(sc_done, n + 1)
                if n >= 3:
                    act.wait_ge(pt_done, n - 2)
                if UNITS[n][0] == "ctx":
                    dst, src = S[n % 3], bank(n % 2)
                else:
                    dst, src = S[n % 3][:, PAST:HALF], bank(6 + n % 2)[:, 0:PAST]
                act.activation(dst, src, ACT.Copy, scale=SCALE).then_inc(s_scaled, 1)

            def exponents(n):
                act.wait_ge(max_done, n + 1)
                parts = 4 if UNITS[n][0] == "ctx" else 1
                for i in range(parts):
                    v = S[n % 3][:, i * (HALF // parts):(i + 1) * (HALF // parts)]
                    act.activation(v, v, ACT.Exp, bias=NMAX[:, n % 3, i:i + 1], accum_out=RSUM[:, n % 3, i:i + 1]
                                   ).then_inc(exp_done, 1)

            def take_turned(n):
                act.wait_ge(pt_done, n + 1)
                if n >= 2:
                    act.wait_ge(pv_done, n - 1)
                act.activation(PT[n % 2], bank(2 + n % 2), ACT.Copy).then_inc(pt_out, 1)

            def take_out(n):
                kind, a, j, par = UNITS[n]
                if kind == "lat" and par == 0:
                    return
                act.wait_ge(pv_done, n + 1)
                src = bank(4 + out_block(n) % 2)
                if kind == "ctx":
                    own = slice(HD * a, HD * a + HD)
                    act.activation(YNA[own, :, 0:CTX], src[own].rearrange("p (a b) -> p a b", a=4),
                                   ACT.Copy).then_inc(po_out, 1)
                else:
                    dst = YNA[:, a, CTX:NT].rearrange("p (r c) -> p r c", c=GRID_W)[:, :, j * COL_BLOCK:(j + 1) * COL_BLOCK]
                    act.activation(dst, src[:, 0:P].rearrange("p (r c) -> p r c", c=COL_BLOCK), ACT.Copy
                                   ).then_inc(po_out, 1)

            for n in range(NU + 3):
                if n < NU:
                    scale(n)
                if 1 <= n <= NU:
                    exponents(n - 1)
                if 2 <= n <= NU + 1:
                    take_turned(n - 2)
                if n >= 3:
                    take_out(n - 3)

            def gate_exponents(e):
                act.wait_ge(pick_step, PICKS * e + SUB_AT)
                act.activation(SMAX, SMAX, ACT.Exp).then_inc(gexp_done, 1)

            for s, (t0, n_tok) in enumerate(SECTIONS):
                for i in range(8):
                    d = 8 * s + i
                    act.wait_ge(gates_done, d + 1)
                    if d >= 2:
                        act.wait_ge(merge_step, 2 * (d - 1))
                    if d == 8:
                        act.wait_ge(pick_step, PICKS)
                    src = bank(4 * (d % 2), 2).rearrange("p (a b) -> p a b", a=2)[:, :, 0:n_tok]
                    act.activation(SG[d % 2][:, :, 0:n_tok], src, ACT.Sigmoid).then_inc(sig_out, 1)
                tiles = (0,) if s == 0 else (1, 2, 3, 4)
                for e in tiles:
                    act.wait_ge(ln_step, LNS * e + 6)
                    act.activation(RSTD[:, 0:1], MV[:, 1:2], ACT.Sqrt).then_inc(sqrt_done, 1)
                    act.wait_ge(ut_done, e + 1)
                    act.activation(UT[:, :, e * P:(e + 1) * P], bank(4 + 2 * (e % 2), 2).rearrange("p (k t) -> p k t", t=P),
                                   ACT.Copy).then_inc(ut_out, 1)
                for f in range(16 * s, 16 * s + 16):
                    act.wait_ge(q_done, f + 1)
                    qg = f // 4
                    if qg >= 1:
                        act.wait_ge(ss_done, qg if s == 0 or qg == 4 else 4 + 4 * (qg - 4))
                    act.activation(QT[:, f % 4, 0:n_tok], bank(f % 2)[:, 0:n_tok], ACT.Copy).then_inc(q_out, 1)
                if s == 0:
                    gate_exponents(0)

            def deviation(e):
                act.wait_ge(fin_step, FIN * e + 6)
                act.activation(RSTD[:, 0:1], MV[:, 1:2], ACT.Sqrt).then_inc(fsqrt_done, 1)

            for e in range(TILES):
                if e + 1 < TILES:
                    gate_exponents(e + 1)
                act.wait_ge(dots_out, GROUPS * (e + 1))
                if e >= 1:
                    act.wait_ge(rank_done, 2 * e)
                act.activation(WTOK, DOTS[e % 2], ACT.Gelu).then_inc(gelu_done, 1)
                for n, (dst, b) in enumerate(((EIDT[e % 2], 2), (WT[e % 2], 3))):
                    act.wait_ge(rank_done, 2 * e + n + 1)
                    if e >= 2:
                        act.wait_ge(v_free, HK * (e - 1) + GROUP)
                    act.activation(dst.rearrange("p (i j) -> p j i", j=4),
                                   bank(b)[:, 0:P].rearrange("p (j i) -> p j i", j=4), ACT.Copy).then_inc(rank_out, 1)
                if e >= 1:
                    deviation(e - 1)
            deviation(TILES - 1)

        @block.vector
        def _(dve):
            def layer_norm(step, base, out, gain, shift, sqrt_sem, sqrt_count):
                for hf in range(2):
                    dve.bn_stats(STAT[:, 6 * hf:6 * hf + 6], out[:, hf * HALF:(hf + 1) * HALF]).then_inc(step, 1)
                dve.wait_ge(step, base + 2)
                dve.bn_aggr(MV, STAT).then_inc(step, 1)
                dve.wait_ge(step, base + 3)
                dve.tensor_scalar(MV[:, 1:2], MV[:, 1:2], EPS, None, ALU.add).then_inc(step, 1)
                dve.wait_ge(sqrt_sem, sqrt_count)
                dve.reciprocal(RSTD[:, 1:2], RSTD[:, 0:1]).then_inc(step, 1)
                dve.wait_ge(step, base + 5)
                dve.tensor_scalar(out, out, MV[:, 0:1], RSTD[:, 1:2], ALU.subtract, ALU.mult).then_inc(step, 1)
                dve.wait_ge(step, base + 6)
                dve.tensor_tensor(out, out, gain, ALU.mult).then_inc(step, 1)
                dve.wait_ge(step, base + 7)
                dve.tensor_tensor(out, out, shift, ALU.add).then_inc(step, 1)

            dve.memset(ZERO, 0.0).then_inc(zero_set, 1)
            dve.wait_ge(silu_step, 1)
            dve.tensor_tensor(SIL, SIL, CT2, ALU.mult).then_inc(silu_step, 1)
            dve.wait_ge(bada_in, 16)

            def add_mods(g):
                dve.wait_ge(ada_done, g + 1)
                own = MODS[:, g * HALF:(g + 1) * HALF]
                dve.tensor_tensor(own, own, bank(6 + g % 2)[0:2, :], ALU.add).then_inc(mod_added, 1)

            for g in range(4):
                add_mods(g)
            dve.wait_ge(mod_added, 4)
            dve.tensor_scalar(MODS[:, D:2 * D], MODS[:, D:2 * D], 1.0, None, ALU.add).then_inc(mod_added, 1)
            dve.wait_ge(modt_done, 1)
            dve.tensor_copy(MODT, bank(5)[:, 0:32].rearrange("p (a b) -> p a b", b=2)).then_inc(modt_ready, 1)
            dve.wait_ge(modt_ready, 1)
            dve.wait_ge(x_in, 16 * KD)
            for k in range(KD):
                for s, (t0, n_tok) in enumerate(SECTIONS):
                    v = UT[:, k, t0:t0 + n_tok]
                    dve.tensor_scalar(v, v, MODT[:, KD + k, s:s + 1], MODT[:, k, s:s + 1], ALU.mult, ALU.add
                                      ).then_inc(u_ready, 1)
            for g in range(4, 10):
                add_mods(g)
            dve.wait_ge(proj_out, 12)
            dve.wait_ge(consts_in, 80)
            dve.tensor_tensor(Aq, Aq, Bk, ALU.mult).then_inc(conv_step, 1)
            dve.wait_ge(conv_step, 1)
            for c in range(4):
                dve.tensor_scalar(CT[:, c, :], Aq[:, c, :], CONVW[:, c, 1:2], None, ALU.mult).then_inc(conv_step, 1)
            dve.wait_ge(conv_step, 5)
            for c in range(4):
                for t0, n_tok in SECTIONS:
                    o = CT[:, c, t0 + 1:t0 + n_tok]
                    dve.scalar_tensor_tensor(o, Aq[:, c, t0:t0 + n_tok - 1], CONVW[:, c, 0:1], o, ALU.mult, ALU.add
                                             ).then_inc(conv_step, 1)
            dve.wait_ge(conv_step, 13)
            for c in range(4):
                for t0, n_tok in SECTIONS:
                    o = CT[:, c, t0:t0 + n_tok - 1]
                    dve.scalar_tensor_tensor(o, Aq[:, c, t0 + 1:t0 + n_tok], CONVW[:, c, 2:3], o, ALU.mult, ALU.add
                                             ).then_inc(conv_step, 1)
            dve.wait_ge(conv_step, 21)
            dve.tensor_tensor(Cy, Cy, CT, ALU.mult).then_inc(conv_step, 1)
            for g in range(10, 12):
                add_mods(g)
            dve.wait_ge(mod_added, 13)
            dve.tensor_scalar(MODS[:, 4 * D:5 * D], MODS[:, 4 * D:5 * D], 1.0, None, ALU.add).then_inc(mod_added, 1)

            def window(n):
                kind, a, j, par = UNITS[n]
                if kind == "lat":
                    if n == 2:
                        dve.wait_ge(bias_in, 16 * ROWS * HEADS)
                    dve.wait_ge(sc_done, n + 1)
                    if n >= 3:
                        dve.wait_ge(pt_done, n - 2)
                    h = 2 * a + par
                    off = BAND_START[j] - j * COL_BLOCK + COL_BLOCK
                    v = S[n % 3][:, 0:PAST].rearrange("p (r c) -> p r c", c=COL_BAND)
                    dve.scalar_tensor_tensor(v, bank(n % 2)[:, 0:PAST].rearrange("p (r c) -> p r c", c=COL_BAND), SCALE,
                                             WB[:, h, :, off:off + COL_BAND], ALU.mult, ALU.add).then_inc(win_step, 1)
                    dve.wait_ge(win_step, 2 * (n - 2) + 1)
                    mask = MASK[:, MASK_OF[j]:MASK_OF[j] + 1, :].to_broadcast([P, ROWS, COL_BAND])
                    dve.tensor_tensor(v, v, mask, ALU.add).then_inc(win_step, 1)
                    dve.wait_ge(win_step, 2 * (n - 1))
                dve.wait_ge(s_scaled, n + 1)
                parts = 4 if kind == "ctx" else 1
                dve.tensor_reduce(NMAX[:, n % 3, 0:parts], S[n % 3].rearrange("p (a b) -> p a b", a=parts), AX, ALU.max,
                                  negate=True).then_inc(max_done, 1)

            def normalise(n):
                parts = 4 if UNITS[n][0] == "ctx" else 1
                dve.wait_ge(exp_done, exps_upto(n))
                dve.reciprocal(RINV[:, n % 3, 0:parts], RSUM[:, n % 3, 0:parts]).then_inc(recip_done, 1)
                dve.wait_ge(recip_done, n + 1)
                for i in range(parts):
                    v = S[n % 3][:, i * (HALF // parts):(i + 1) * (HALF // parts)]
                    dve.tensor_scalar(v, v, RINV[:, n % 3, i:i + 1], None, ALU.mult).then_inc(norm_done, 1)

            for n in range(NU + 1):
                if n < NU:
                    window(n)
                if n >= 1:
                    normalise(n - 1)

            def route(e, part):
                base = PICKS * e
                val = VAL[:, e, :].rearrange("p (h s k) -> p h s k", s=2, k=TOPK)
                idxf = IDXF.rearrange("p (h s k) -> p h s k", s=2, k=TOPK)
                cube = [P, PEER_HEADS, TOPK, TOPK]
                if part == 0:
                    dve.wait_ge(topk_step, 80 if e == 0 else 400)
                    if e >= 1:
                        dve.wait_ge(pick_step, base)
                step = [base if part == 0 else base + SUB_AT]

                def done(ins):
                    step[0] += 1
                    ins.then_inc(pick_step, 1)

                def settle():
                    dve.wait_ge(pick_step, step[0])

                cands = CANDS.rearrange("p h (a b) -> p h a b", b=TOPK)
                eq = EQ.rearrange("p h (a b) -> p h a b", b=TOPK)
                pos = POS.rearrange("p (h k) -> p h k", k=TOPK)
                smax = SMAX.rearrange("p (h k) -> p h k", k=TOPK)
                if part == 0:
                    done(dve.tensor_tensor(cands, val[:, :, 0, :].unsqueeze(3).to_broadcast(cube),
                                           val[:, :, 1, :].unsqueeze(2).to_broadcast(cube), ALU.add))
                    done(dve.tensor_copy(IDXF, IDXS[e]))
                    settle()
                    for lo in (0, 8):
                        for h in range(PEER_HEADS):
                            done(dve.max(TOPS[:, h, lo:lo + 8], CANDS[:, h, :]))
                        settle()
                        for h in range(PEER_HEADS):
                            done(dve.max_index(pos[:, h, lo:lo + 8], TOPS[:, h, lo:lo + 8], CANDS[:, h, :]))
                        settle()
                        if lo == 0:
                            for h in range(PEER_HEADS):
                                done(dve.match_replace(CANDS[:, h, :], TOPS[:, h, 0:8], CANDS[:, h, :], LOWEST))
                            settle()
                    done(dve.tensor_tensor(smax, TOPS, TOPS[:, :, 0:1].to_broadcast([P, PEER_HEADS, TOPK]), ALU.subtract))
                    assert step[0] == base + SUB_AT
                    return
                done(dve.tensor_scalar(PA, POS, 4, None, ALU.logical_shift_right))
                done(dve.tensor_scalar(PB, POS, TOPK - 1, None, ALU.bitwise_and))
                settle()
                done(dve.tensor_copy(AF, PA))
                done(dve.tensor_copy(BF, PB))
                settle()
                iota = IOTA.unsqueeze(1).unsqueeze(1).to_broadcast(cube)
                for side, digit, res in ((0, AF, I0), (1, BF, I1)):
                    d4 = digit.rearrange("p (h k) -> p h k", k=TOPK).unsqueeze(3).to_broadcast(cube)
                    done(dve.tensor_tensor(eq, d4, iota, ALU.is_equal))
                    settle()
                    done(dve.tensor_tensor(eq, eq, idxf[:, :, side, :].unsqueeze(2).to_broadcast(cube), ALU.mult))
                    settle()
                    done(dve.tensor_reduce(res.rearrange("p (h k) -> p h k", k=TOPK), eq, AX, ALU.add))
                    settle()
                done(dve.scalar_tensor_tensor(EID[:, e, :], I0, float(NKEYS), I1, ALU.mult, ALU.add))
                if e >= 2:
                    dve.wait_ge(rank_done, 2 * e - 3)
                done(dve.scalar_tensor_tensor(EIDF[e % 2], I0, float(NKEYS), I1, ALU.mult, ALU.add))
                dve.wait_ge(gexp_done, e + 1)
                done(dve.tensor_reduce(GSUM, smax, AX, ALU.add))
                settle()
                done(dve.reciprocal(GSUM, GSUM))
                settle()
                done(dve.tensor_tensor(GATE[:, e, :].rearrange("p (h k) -> p h k", k=TOPK), smax,
                                       GSUM.unsqueeze(2).to_broadcast([P, PEER_HEADS, TOPK]), ALU.mult))
                assert step[0] == base + PICKS, step[0] - base

            IDXS = [IDX] + [at(33792 + 256 * i, 2 * PEER_HEADS * TOPK).bitcast(U32) for i in range(4)]

            for s, (t0, n_tok) in enumerate(SECTIONS):
                tiles = (0,) if s == 0 else (1, 2, 3, 4)
                for i in range(8):
                    d = 8 * s + i
                    sg = SG[d % 2][:, :, 0:n_tok]
                    dve.wait_ge(sig_out, d + 1)
                    dve.wait_ge(merge_done, d + 1)
                    dve.tensor_tensor(sg, sg, bank(4 * (d % 2) + 2, 2).rearrange("p (a b) -> p a b", a=2)[:, :, 0:n_tok],
                                      ALU.mult).then_inc(merge_step, 1)
                    dve.wait_ge(merge_step, 2 * d + 1)
                    dve.tensor_tensor(MT[:, i, 0:n_tok], sg[:, 0, :], sg[:, 1, :], ALU.add).then_inc(merge_step, 1)
                for e in tiles:
                    base = LNS * e
                    xr, xb, u2 = XR[e % 2], XB[e % 2], U2[e % 2]
                    dve.wait_ge(wo_done, e + 1)
                    dve.wait_ge(prm_in[s], 80 if s == 0 else 48)
                    if e >= 2:
                        dve.wait_ge(store_out[e % 2], 32 * (e // 2))
                    dve.tensor_tensor(xr, bank(2 * (e % 2), 2), PRM[0], ALU.mult).then_inc(ln_step, 1)
                    dve.wait_ge(ln_step, base + 1)
                    dve.wait_ge(xb_in[e % 2], 16 * (e // 2 + 1))
                    dve.scalar_tensor_tensor(xr, xb, ALPHA, xr, ALU.mult, ALU.add).then_inc(ln_step, 1)
                    dve.wait_ge(ln_step, base + 2)
                    layer_norm(ln_step, base + 2, xr, PRM[1], PRM[2], sqrt_done, e + 1)
                    dve.wait_ge(ln_step, base + 10)
                    dve.tensor_tensor(u2, xr, PRM[3], ALU.mult).then_inc(ln_step, 1)
                    dve.wait_ge(ln_step, base + 11)
                    dve.tensor_tensor(u2, u2, PRM[4], ALU.add).then_inc(ln_step, 1)
                for qg in range(4):
                    for tl, e in enumerate(tiles):
                        si = qg if s == 0 else 4 + 4 * qg + tl
                        idx = IDXS[e]
                        dve.wait_ge(ss_done, si + 1)
                        if si >= 1:
                            dve.wait_ge(topk_step, 20 * si)
                        sc = bank(2 + si % 2)
                        if e >= 1 and qg == 0 and tl == 0:
                            dve.wait_ge(ut_done, TILES)
                            all_stored(dve)

                        def best(c, lo):
                            o = (4 * qg + c) * TOPK + lo
                            return slice(o, o + 8)

                        for lo in (0, 8):
                            for c in range(4):
                                src = sc[:, c * P:(c + 1) * P] if lo == 0 else SW[:, c, :]
                                dve.max(VAL[:, e, best(c, lo)], src).then_inc(topk_step, 1)
                            dve.wait_ge(topk_step, 20 * si + 4 + 12 * (lo // 8))
                            for c in range(4):
                                src = sc[:, c * P:(c + 1) * P] if lo == 0 else SW[:, c, :]
                                dve.max_index(idx[:, best(c, lo)], VAL[:, e, best(c, lo)], src).then_inc(topk_step, 1)
                            if lo == 0:
                                for c in range(4):
                                    dve.match_replace(SW[:, c, :], VAL[:, e, best(c, 0)], sc[:, c * P:(c + 1) * P], LOWEST
                                                      ).then_inc(topk_step, 1)
                                dve.wait_ge(topk_step, 20 * si + 12)
                if s == 0:
                    route(0, 0)
                    route(0, 1)

            def finish(e):
                base = FIN * e
                yr = YR[e % 2]
                dve.wait_ge(y_done, e + 1)
                dve.wait_ge(prm2_in, 48 if e == 0 else 64)
                dve.wait_ge(x1_in[e % 2], 16 * (e // 2 + 1))
                if e >= 2:
                    dve.wait_ge(y_out[e % 2], 16 * (e // 2))
                dve.tensor_tensor(yr, bank(4 + 2 * (e % 2), 2), PRM2[0], ALU.mult).then_inc(fin_step, 1)
                dve.wait_ge(fin_step, base + 1)
                dve.scalar_tensor_tensor(yr, X1B[e % 2], ALPHA, yr, ALU.mult, ALU.add).then_inc(fin_step, 1)
                dve.wait_ge(fin_step, base + 2)
                layer_norm(fin_step, base + 2, yr, PRM2[1], PRM2[2], fsqrt_done, e + 1)

            dve.memset(DOT, 0.0).then_inc(u_free, GROUP)
            dve.wait_ge(u_free, GROUP)

            def groups(e, lo, hi):
                with dve.Fori(lo, hi) as g:
                    for b in range(GROUP):
                        dve.wait_ge(u_land[b], 16 * GROUPS * e + 16 * g + 16)
                        dve.tensor_tensor_reduce(UR[b], UR[b], U2B[e % 2], 1.0, 0.0, ALU.mult, ALU.add,
                                                 DOT[:, b:b + 1]).then_inc(u_free, 1)
                    dve.wait_ge(u_free, GROUP * g + (HK * e + 2 * GROUP))
                    dve.tensor_copy(DOTS[e % 2][:, bass.ds(GROUP * g, GROUP)], DOT).then_inc(dots_out, 1)
                    dve.wait_ge(dots_out, GROUPS * e + g + 1)

            for e in range(TILES):
                dve.wait_ge(u2_in[e % 2], 16 * (e // 2 + 1))
                groups(e, 0, 4)
                if e >= 2:
                    finish(e - 2)
                if e + 1 < TILES:
                    groups(e, 4, 7)
                    route(e + 1, 0)
                    groups(e, 7, 11)
                    route(e + 1, 1)
                    groups(e, 11, GROUPS)
                else:
                    groups(e, 4, GROUPS)
                dve.wait_ge(gelu_done, e + 1)
                dve.tensor_tensor(WTOK, WTOK, GATE[:, e, :], ALU.mult).then_inc(weighed, 1)
            finish(TILES - 2)
            finish(TILES - 1)


LNS = 12
FIN = 10
SUB_AT = 2 + 5 * PEER_HEADS + 1
PICKS = SUB_AT + 4 + 6 + 5

_OUTS = [((1, CTX, D), "y_prompt"), ((1, LAT, D), "y_sample"), ((1, 1, CTX, HEADS, HD), "new_k"),
         ((1, 1, CTX, HEADS, HD), "new_v")]


def kernel(**inputs):
    import numpy as _np
    import concourse.bacc as _bacc
    from concourse import mybir as _mybir
    from concourse.bass_utils import run_bass_kernel_spmd as _run

    i = {k: _np.asarray(v) for k, v in inputs.items()}
    xs = _np.concatenate([i["x_prompt"][0], i["x_sample"][0]], axis=0)
    rpb = _np.pad(i["rpb"].reshape(-1), (16, 16))
    laid = {
        "x_prompt": i["x_prompt"], "x_sample": i["x_sample"], "xT": xs.T,
        "ck_T": i["cache_k"][0, 0].reshape(PAST, HEADS * HD).T, "cache_v": i["cache_v"],
        "c_T": _np.stack([i["c_ctx"], i["c"][0]], axis=-1).reshape(KD, P, 2).transpose(1, 0, 2),
        "w_ada": i["w_ada"], "b_ada": i["b_ada"], "w_in": i["w_in"],
        "convw_T": i["conv_w"][0].reshape(3, 4, P).transpose(2, 1, 0),
        "w_conv_out": i["w_conv_out"], "w_na_out": i["w_na_out"],
        "rpb_rows": _np.stack([rpb[15 - q:15 - q + rpb.size - 15] for q in range(COL_BLOCK)]),
        "w_o": i["w_o"], "ln1_g": i["ln1_g"], "ln1_b": i["ln1_b"], "w_query": i["w_query"],
        "sub_keys_T": i["sub_keys"][0].reshape(2 * PEER_HEADS, NKEYS, P).transpose(2, 0, 1),
        "expert_u": i["expert_u"], "expert_v": i["expert_v"], "ln2_g": i["ln2_g"], "ln2_b": i["ln2_b"],
        "ident_in": _np.eye(P, dtype=_np.float32), "mask_in": window_mask(),
        "iota_in": _np.tile(_np.arange(TOPK, dtype=_np.float32), (P, 1)),
        "pickrow_in": _np.eye(QUAD, dtype=_np.float32).reshape(1, QUAD, QUAD),
    }
    nc = _bacc.Bacc("TRN2", target_bir_lowering=False, num_devices=1)
    arrays, args = {}, []
    for name, a in laid.items():
        a = _np.ascontiguousarray(a)
        arrays[f"in_{name}_dram"] = a
        args.append(nc.dram_tensor(f"in_{name}_dram", a.shape, _mybir.dt.from_np(a.dtype), kind="ExternalInput").ap())
    for shape, name in _OUTS:
        args.append(nc.dram_tensor(f"out_{name}_dram", shape, F32, kind="ExternalOutput").ap())
    backbone(nc, *args)
    r = _run(nc, [arrays], core_ids=[0])
    return tuple(r.results[0][f"out_{name}_dram"] for _, name in _OUTS)
```

```python
from contextlib import ExitStack

import numpy as np

import concourse.bass as bass
from concourse import mybir

ALU = mybir.AluOpType
ACT = mybir.ActivationFunctionType
AX = mybir.AxisListType.X
F32 = mybir.dt.float32
U32 = mybir.dt.uint32

P = 128
D = 1024
KD = D // P
CTX, LAT = 128, 512
NT = CTX + LAT
TILES = NT // P
SECTIONS = ((0, CTX), (CTX, LAT))
GRID_W, ROWS = 64, 8
PAST = 256
HEADS, HD = 8, 64
WIN_W, COL_BLOCK, COL_BAND = 16, 16, 32
WIDE = COL_BLOCK + COL_BAND
BLOCKS = GRID_W // COL_BLOCK
RPB_H, RPB_W = 15, 31
PEER_HEADS, TOPK, NKEYS = 8, 16, 128
HK = PEER_HEADS * TOPK
CAND = TOPK * TOPK
GROUP = 8
GROUPS = HK // GROUP
SCALE = HD ** -0.5
ALPHA = 2.0 ** 0.25
EPS = 1e-5
NEG = -1e30
LOWEST = -3.0e38
HALF = 512
MERGE = ("gconv", "gna", "branch")
WSLOTS = 3
SUMMED_LATE = (3, 4)
QUAD = P // 4
LAG = 2

BAND_START = [min(max(j * COL_BLOCK - WIN_W // 2, 0), GRID_W - COL_BAND) for j in range(BLOCKS)]
MASK_OF = [0, 1, 1, 2]


def window_mask():
    m = np.zeros((P, 3, COL_BAND), np.float32)
    for j in (0, 1, 3):
        for p in range(P):
            q = j * COL_BLOCK + p % COL_BLOCK
            start = min(max(q - WIN_W // 2, 0), GRID_W - WIN_W)
            cols = BAND_START[j] + np.arange(COL_BAND)
            m[p, MASK_OF[j], (cols < start) | (cols >= start + WIN_W)] = NEG
    return m.reshape(P, 3 * COL_BAND)


def weight_loads():
    loads = [("ada", g) for g in range(4)]
    for n, g in enumerate(PROJ):
        loads.append(("in", 0, g))
        if n < 4:
            loads += [("ada", 4 + 2 * n), ("ada", 5 + 2 * n)]
    for s in range(2):
        if s == 1:
            loads += [("in", 1, g) for g in PROJ]
        for hf in range(2):
            loads += [("gconv", s, hf), ("gna", s, hf), ("branch", s, hf)]
        loads += [("out", s, 0), ("out", s, 1)]
        loads += [("query", s, g) for g in range(4)]
    return loads


PROJ = (0, 2, 1, 5, 3, 4)
PROJ_AT = tuple(range(6)) + tuple(6 + 4 * n for n in range(7))
PROJ_CTX, PROJ_ALL = 6, PROJ_AT[-1]


def mod_adds(g):
    return g + 1 if g < 4 else g + 2


def units():
    out = [("ctx", b, 0, 0) for b in range(2)]
    out += [("lat", hp, j, par) for hp in range(HEADS // 2) for j in range(BLOCKS) for par in range(2)]
    return out


UNITS = units()
NU = len(UNITS)


def exps_upto(n):
    return 4 * (n + 1) if n < 2 else 8 + (n - 1)


def outputs_upto(n):
    return n + 1 if n < 2 else 2 + (n - 1) // 2


def out_block(n):
    return n if n < 2 else 2 + (n - 2) // 2


def backbone(nc, x_prompt, x_sample, xT, ck_T, cache_v, c_T, w_ada, b_ada, w_in, convw_T, w_conv_out,
             w_na_out, rpb_rows, w_o, ln1_g, ln1_b, w_query, sub_keys_T, expert_u, expert_v, ln2_g, ln2_b,
             ident_in, sel_in, mask_in, iota_in, pickrow_in,
             y_prompt, y_sample, new_k, new_v):
    mods_d = nc.dram_tensor("mods_d", (2, 6 * D), F32, kind="Internal").ap()
    x1_d = nc.dram_tensor("x1_d", (NT, D), F32, kind="Internal").ap()
    u2_d = nc.dram_tensor("u2_d", (NT, D), F32, kind="Internal").ap()

    def rows(prompt, sample, e):
        return prompt[0] if e == 0 else sample[0, (e - 1) * P:e * P, :]

    with ExitStack() as ctx:
        def sem(name):
            return ctx.enter_context(nc.semaphore(name))

        arena = ctx.enter_context(nc.sbuf_tensor("arena", [P, 53184], F32))
        psum = ctx.enter_context(nc.psum_tensor("psum", [P, 8 * HALF], F32))

        def bank(b, n=1):
            return psum[:, b * HALF:(b + n) * HALF]

        def at(off, *shape):
            n = int(np.prod(shape))
            v = arena[:, off:off + n]
            if len(shape) == 2:
                v = v.rearrange("p (a b) -> p a b", b=shape[1])
            if len(shape) == 3:
                v = v.rearrange("p (a b c) -> p a b c", b=shape[1], c=shape[2])
            return v

        W = [at(4096 * i, KD, HALF) for i in range(WSLOTS)] + [at(31744, KD, HALF)]
        UR = [at(12288 + 1024 * i, D) for i in range(GROUP)]
        UT = at(20480, KD, NT)
        Aq, Bk, Cy = at(25600, 4, NT), at(28160, 4, NT), at(30720, 4, NT)
        YNA = [at(33280, 4, CTX), at(33792, 4, LAT)]
        CT = [at(33792, 4, CTX), at(35840, 4, LAT)]
        VB = at(35840, 2 * BLOCKS, HALF)
        MODS = at(35840, 6 * D)[0:2, :]
        SILP = at(12288, KD, QUAD)
        PARTS4 = [at(12544 + HALF * i, HALF) for i in range(2)]
        CK = at(39936, 4, PAST)
        CV = at(40960, 2, HALF)
        WB = at(41984, HEADS, ROWS, WIDE)
        SK = at(45056, 2 * PEER_HEADS, NKEYS)
        V = [at(17408, 1, HALF), at(33792, TILES - 1, HALF)]
        KTOK = at(17920, HALF)
        S = [[at(12288 + HALF * i, HALF) for i in range(2)], [at(8192 + HALF * i, HALF) for i in range(3)]]
        PT = [[at(13312 + HALF * i, HALF) for i in range(2)], [at(10240 + HALF * i, HALF) for i in range(2)]]
        PRM = [[at(12288 + 1024 * i, D) for i in range(5)],
               [at(35840 + 1024 * i, D) for i in range(5)]]
        XB = [at(17408, D), at(43008, D)]
        SG = [at(35328, 2, CTX), at(44032, 2, LAT)]
        MT = [at(33792, KD, CTX), at(25600, KD, LAT)]
        QT = [[at(o + 4 * P * i, 4, P) for i in range(2)] for o in (34816, 25600)]
        XR = [at(18432, D)] + [at(40960 + 1024 * (e % 2), D) for e in range(1, TILES)]
        U2 = [at(19456, D)] + [at(29696 + 1024 * (e % 2), D) for e in range(1, TILES)]
        CANDS = [at(12288 if e == 0 else 29696, PEER_HEADS, CAND) for e in range(TILES)]
        EQ = [at(14336 if e == 0 else 40960, PEER_HEADS, CAND) for e in range(TILES)]
        LATE = {e: at(35840 + 2048 * i, 4, HALF) for i, e in enumerate(SUMMED_LATE)}
        VR = [UR] + [[at(1024 * i, D) for i in range(GROUP)]] * (TILES - 1)
        U2B = [at(47104, D), at(43008, D)] + [at(20480 + 1024 * (e % 2), D) for e in range(2, TILES)]
        X1B = [at(22528 + 1024 * i, D) for i in range(2)]
        PRM2 = [at(24576, D), at(31744, D), at(32768, D)]
        YR = [at(33792 + 1024 * i, D) for i in range(2)]
        small = [47104]

        def keep(*shape):
            v = at(small[0], *shape)
            small[0] += int(np.prod(shape))
            return v

        VAL = [keep(2 * PEER_HEADS * TOPK)] + [at(27648 + 256 * i, 2 * PEER_HEADS * TOPK) for i in range(TILES - 1)]
        IDXS = [keep(2 * PEER_HEADS * TOPK).bitcast(U32)] + [at(28672 + 256 * i, 2 * PEER_HEADS * TOPK).bitcast(U32)
                                                             for i in range(TILES - 1)]
        SW = keep(4, NKEYS)
        IDN, ZERO, PICKROW = keep(P), keep(HALF), keep(QUAD, QUAD)
        IDXF = keep(2 * PEER_HEADS * TOPK)
        EID, EIDF = [keep(HK).bitcast(U32) for _ in range(2)], [keep(HK) for _ in range(2)]
        EIDT = [keep(P).bitcast(U32) for _ in range(2)]
        WT = [keep(P) for _ in range(2)]
        GATE, WTOK, DOTS = [keep(HK) for _ in range(2)], keep(HK), [keep(HK) for _ in range(2)]
        WCOL = [keep(4, QUAD), keep(4, QUAD)]
        LAST_COLS = [at(44032, 4, QUAD), at(44160, 4, QUAD)] + WCOL
        DOT, NUM = keep(GROUP), [keep(GROUP).bitcast(U32) for _ in range(2)]
        MODT, CONVW, MASK, IOTA = keep(16, 2), keep(4, 3), keep(3, COL_BAND), keep(TOPK)
        CT2, SIL, SEL = keep(KD, 2), keep(KD, 2), keep(2)
        NMAX, RSUM, RINV = keep(3, 4), keep(3, 4), keep(3, 4)
        STAT, MV, RSTD = keep(12), keep(2), keep(2)
        SMAX, TOPS, GSUM = keep(HK), keep(PEER_HEADS, TOPK), keep(PEER_HEADS)
        POS, PA, AF, BF = keep(HK).bitcast(U32), keep(HK).bitcast(U32), keep(HK), keep(HK)
        assert small[0] <= 53184, small[0]

        w_land = [sem(f"w_land{i}") for i in range(WSLOTS + 1)]
        part_land = [[sem(f"{kind}_land{c}") for c in range(4)] for kind in MERGE]
        consts_in, x_in, bias_in, ctx_in = sem("consts_in"), sem("x_in"), sem("bias_in"), sem("ctx_in")
        bada_in, keys_in = sem("bada_in"), sem("keys_in")
        cond_in, ada_out, ada_summed = sem("cond_in"), sem("ada_out"), sem("ada_summed")
        silu_step, ada_done, mod_added, modt_done, modt_ready = (
            sem("silu_step"), sem("ada_done"), sem("mod_added"), sem("modt_done"), sem("modt_ready"))
        u_ready, mods_out = sem("u_ready"), sem("mods_out")
        proj_done, proj_out, conv_step = sem("proj_done"), sem("proj_out"), sem("conv_step")
        kt_done, kt_out, cache_out, band_in = sem("kt_done"), sem("kt_out"), sem("cache_out"), sem("band_in")
        sc_done, s_scaled, win_step, max_done, exp_done = (
            sem("sc_done"), sem("s_scaled"), sem("win_step"), sem("max_done"), sem("exp_done"))
        recip_done, norm_done, pt_done, pt_out, pv_done, po_out = (
            sem("recip_done"), sem("norm_done"), sem("pt_done"), sem("pt_out"), sem("pv_done"), sem("po_out"))
        gates_done, merge_done, sig_out, merge_step = (
            sem("gates_done"), sem("merge_done"), sem("sig_out"), sem("merge_step"))
        prm_in = [sem("prm_in0"), sem("prm_in1")]
        xb_in = sem("xb_in")
        store_out = [sem("store_out0"), sem("store_out1")]
        wo_done, ln_step, sqrt_done, ut_done, ut_out = (
            sem("wo_done"), sem("ln_step"), sem("sqrt_done"), sem("ut_done"), sem("ut_out"))
        q_done, q_out, ss_done, ss_out, topk_step, pick_step, gexp_done = (
            sem("q_done"), sem("q_out"), sem("ss_done"), sem("ss_out"), sem("topk_step"), sem("pick_step"), sem("gexp_done"))
        x1_in, u2_in = [sem("x1_in0"), sem("x1_in1")], [sem("u2_in0"), sem("u2_in1")]
        prm2_in, u_land, v_land = sem("prm2_in"), [sem(f"u_land{i}") for i in range(GROUP)], [
            sem(f"v_land{i}") for i in range(GROUP)]
        num_ready, u_free, v_free, dots_out, cols_ready = (
            sem("num_ready"), sem("u_free"), sem("v_free"), sem("dots_out"), sem("cols_ready"))
        gelu_done, weighed, rank_done, rank_out = sem("gelu_done"), sem("weighed"), sem("rank_done"), sem("rank_out")
        zero_set, y_done, fin_step, fsqrt_done = (
            sem("zero_set"), sem("y_done"), sem("fin_step"), sem("fsqrt_done"))
        y_out = [sem("y_out0"), sem("y_out1")]
        pick_in, ctx_u2_in = sem("pick_in"), sem("ctx_u2_in")

        loads = weight_loads()
        slot_of, before, last, counts, landed = {}, {}, {}, [0] * (WSLOTS + 1), {}
        for n, key in enumerate(loads):
            slot = n % WSLOTS
            if key[0:2] == ("query", 1):
                slot = (2, 3, 0, 1)[key[2]]
            slot_of[key], before[key], last[slot] = slot, last.get(slot), key
            if key[0] in MERGE and key[2] == 1:
                continue
            counts[slot] += 32 if key[0] == "branch" else 16
            landed[key] = counts[slot]

        def freed_by(key):
            kind = key[0]
            if kind == "ada":
                return ada_done, key[1] + 1
            if kind == "in":
                return proj_done, PROJ_AT[6 * key[1] + PROJ.index(key[2]) + 1]
            if kind in MERGE:
                return merge_done if kind == "branch" else gates_done, 8 * key[1] + 4 * key[2] + 4
            if kind == "out":
                return wo_done, 1 if key[1] == 0 else TILES
            return q_done, key[2] + 1

        def weights(pe, key):
            pe.wait_ge(w_land[slot_of[key]], landed[key])
            return W[slot_of[key]]

        def merge_weights(pe, kind, s, hf, c):
            if hf == 0:
                return weights(pe, (kind, s, 0))
            pe.wait_ge(part_land[MERGE.index(kind)][c], (32 if kind == "branch" else 16) * (s + 1))
            return W[slot_of[kind, s, 1]]

        def s_buf(n):
            return S[0][n] if n < 2 else S[1][n % 3]

        def pt_buf(n):
            return PT[0][n] if n < 2 else PT[1][n % 2]

        def w_cols(w, c0, n=HALF):
            return w[:, c0:c0 + n].rearrange("(k p) n -> p k n", p=P)

        def all_stored(eng):
            for i in range(2):
                eng.wait_ge(store_out[i], 32 * len(range(i, TILES, 2)))

        block = ctx.enter_context(nc.Block())

        @block.sync
        def _(sp):
            def load_u2(e):
                if e >= 3:
                    sp.wait_ge(u_free, HK * (e - 1) + GROUP)
                sp.dma_start(U2B[e], u2_d[e * P:(e + 1) * P, :]).then_inc(u2_in[e % 2], 16)

            for key in loads:
                if key == ("gconv", 1, 0):
                    sp.wait_ge(proj_out, PROJ_AT[6 + 4])
                    sp.wait_ge(conv_step, 28)
                    for j in range(BLOCKS):
                        for i in range(ROWS):
                            p0 = (i % 2) * GRID_W + BAND_START[j]
                            sp.dma_start(VB[(i % 4) * COL_BAND:(i % 4 + 1) * COL_BAND, 2 * j + i // 4, :],
                                         V[1][p0:p0 + COL_BAND, i // 2, :]).then_inc(band_in, 16)
                if key == ("branch", 1, 0):
                    sp.wait_ge(po_out, outputs_upto(NU - 1))
                if slot_of[key] == 3:
                    sp.wait_ge(merge_done, 16)
                dst, done = W[slot_of[key]], w_land[slot_of[key]]
                if key[0] in MERGE and key[2] == 1:
                    if key[0] == "gconv":
                        for c in range(4):
                            sp.wait_ge(gates_done, 8 * key[1] + c + 1)
                            cols = slice(c * P, (c + 1) * P)
                            for i, block in ((0, 6), (1, 8)):
                                sp.dma_start(W[i][:, :, cols], w_cols(w_in[0], (block + 1) * HALF + c * P, P)
                                             ).then_inc(part_land[i][c], 16)
                            sp.wait_ge(merge_done, 8 * key[1] + c + 1)
                            for k0, w in ((0, w_conv_out), (4, w_na_out)):
                                sp.dma_start(W[2][:, k0:k0 + 4, cols], w_cols(w[0], HALF + c * P, P)
                                             ).then_inc(part_land[2][c], 16)
                    continue
                if before[key]:
                    sp.wait_ge(*freed_by(before[key]))
                kind = key[0]
                if kind == "ada":
                    sp.dma_start(dst, w_cols(w_ada[0], key[1] * HALF)).then_inc(done, 16)
                elif kind == "in":
                    sp.dma_start(dst, w_cols(w_in[0], key[2] * HALF)).then_inc(done, 16)
                elif kind == "gconv":
                    sp.dma_start(dst, w_cols(w_in[0], (6 + key[2]) * HALF)).then_inc(done, 16)
                elif kind == "gna":
                    sp.dma_start(dst, w_cols(w_in[0], (8 + key[2]) * HALF)).then_inc(done, 16)
                elif kind == "branch":
                    sp.dma_start(dst[:, 0:4, :], w_cols(w_conv_out[0], key[2] * HALF)).then_inc(done, 16)
                    sp.dma_start(dst[:, 4:8, :], w_cols(w_na_out[0], key[2] * HALF)).then_inc(done, 16)
                elif kind == "out":
                    sp.dma_start(dst, w_cols(w_o[0], key[2] * HALF)).then_inc(done, 16)
                else:
                    sp.dma_start(dst, w_cols(w_query[0], key[2] * HALF)).then_inc(done, 16)

            def load_x1(e):
                if e >= 2:
                    sp.wait_ge(fin_step, FIN * (e - 1))
                sp.dma_start(X1B[e % 2], x1_d[e * P:(e + 1) * P, :]).then_inc(x1_in[e % 2], 16)

            def second_gate(s):
                sp.dma_start(PRM2[0], mods_d[s:s + 1, 5 * D:6 * D].partition_broadcast(P)).then_inc(prm2_in, 16)

            def store_y(e):
                sp.wait_ge(fin_step, FIN * (e + 1))
                sp.dma_start(rows(y_prompt, y_sample, e), YR[e % 2]).then_inc(y_out[e % 2], 16)

            all_stored(sp)
            load_u2(1)
            sp.wait_ge(q_done, 4 * TILES)
            load_x1(0)
            load_u2(2)
            load_x1(1)
            sp.dma_start(PRM2[1], ln2_g[0:1, :].partition_broadcast(P)).then_inc(prm2_in, 16)
            sp.dma_start(PRM2[2], ln2_b[0:1, :].partition_broadcast(P)).then_inc(prm2_in, 16)
            second_gate(0)
            store_y(0)
            second_gate(1)
            load_x1(2)
            load_u2(3)
            load_u2(4)
            for e in range(1, TILES):
                store_y(e)
                if e + 2 < TILES:
                    load_x1(e + 2)
            for i in range(2):
                sp.wait_ge(y_out[i], 16 * len(range(i, TILES, 2)))
            sp.wait_ge(cache_out, 32)

        @block.gpsimd
        def _(pool):
            pool.dma_start(MODS, b_ada[0:1, :].partition_broadcast(2)).then_inc(bada_in, 16)
            for k in range(KD):
                pool.dma_start(UT[:, k, :], xT[k * P:(k + 1) * P, :]).then_inc(x_in, 16)
            pool.dma_start(CONVW, convw_T).then_inc(consts_in, 16)
            pool.dma_start(MASK, mask_in.rearrange("p (a b) -> p a b", b=COL_BAND)).then_inc(consts_in, 16)
            pool.dma_start(IOTA, iota_in).then_inc(consts_in, 16)
            pool.dma_start(SK, sub_keys_T).then_inc(keys_in, 16)
            pool.dma_start(PICKROW, pickrow_in.partition_broadcast(P)).then_inc(pick_in, 16)
            length = rpb_rows.shape[1]
            for r in range(ROWS):
                for h in range(HEADS):
                    src = bass.AP(rpb_rows.tensor, h * RPB_H * RPB_W + (ROWS - 1 - r) * RPB_W,
                                  [[length, COL_BLOCK], [RPB_W, ROWS], [1, WIDE]])
                    pool.dma_start(WB[r * COL_BLOCK:(r + 1) * COL_BLOCK, h], src).then_inc(bias_in, 16)
            pool.wait_ge(mod_added, 14)
            pool.dma_start(mods_d, MODS).then_inc(mods_out, 16)
            pool.wait_ge(mods_out, 16)
            for t in range(2):
                pool.dma_start(CV[:, t, :], cache_v[0, 0, t * P:(t + 1) * P].rearrange("t h d -> t (h d)")
                               ).then_inc(ctx_in, 16)
            for c in range(4):
                pool.dma_start(CK[:, c, :], ck_T[c * P:(c + 1) * P, :]).then_inc(ctx_in, 16)
            pool.wait_ge(proj_out, 4)
            pool.dma_start(new_v[0, 0].rearrange("t h d -> t (h d)"), V[0][:, 0, :]).then_inc(cache_out, 16)
            pool.wait_ge(kt_out, 1)
            pool.dma_start(new_k[0, 0].rearrange("t h d -> t (h d)"), KTOK).then_inc(cache_out, 16)

            def fetch(side, table, b0, source, slots):
                own = slice(b0, b0 + 4)
                pool.tensor_copy(NUM[side][:, own], source).then_inc(num_ready, 1)
                pool.wait_ge(num_ready, 1)
                pool.sem_clear(num_ready)
                for b in range(b0, b0 + 4):
                    land = (u_land, v_land)[side][b]
                    pool.indirect_dma_start(slots[b], None, table[0], bass.IndirectOffsetOnAxis(
                        ap=NUM[side][:, b:b + 1], axis=0)).then_inc(land, 16)

            def columns(e, cols, first, row):
                w = WT[e % 2][:, bass.ds(first, 4)]
                pick = PICKROW[:, bass.ds(row, 1), :]
                pool.tensor_tensor(cols, w.unsqueeze(2).to_broadcast([P, 4, QUAD]), pick.to_broadcast([P, 4, QUAD]),
                                   ALU.mult).then_inc(cols_ready, 1)

            def last_sums():
                e = TILES - 1
                pool.wait_ge(u_free, HK * TILES + GROUP)
                with pool.Fori(0, GROUPS // 2) as g:
                    for k in range(4):
                        first, b0 = 2 * GROUP * g + 4 * k, 4 * (k % 2)
                        pool.wait_ge(v_free, 2 * GROUP * g + (HK * e + 4 * k - 4))
                        fetch(k // 2, expert_v, b0, EIDT[e % 2][:, bass.ds(first, 4)], UR if k < 2 else VR[e])
                        pool.wait_ge(rank_out, 2 * e + 2)
                        columns(e, LAST_COLS[k], first, 4 * g + k)

            def stretch(n, u=None, v=None):
                with pool.Fori(0, n) as g:
                    for b0 in (0, 4):
                        if u:
                            e, g0 = u
                            pool.wait_ge(u_free, GROUP * g + (HK * e + GROUP * g0 + b0 + 4))
                            fetch(0, expert_u, b0, EID[e % 2][:, bass.ds(GROUP * g + (GROUP * g0 + b0), 4)], UR)
                        if v:
                            e, g0 = v
                            pool.wait_ge(v_free, GROUP * g + (HK * e + GROUP * g0 + b0 + 4))
                            fetch(1, expert_v, b0, EIDT[e % 2][:, bass.ds(GROUP * g + (GROUP * g0 + b0), 4)], VR[e])
                            pool.wait_ge(rank_out, 2 * e + 2)
                            columns(e, WCOL[b0 // 4], GROUP * g + (GROUP * g0 + b0), 2 * g + (2 * g0 + b0 // 4))

            def routed(e):
                pool.wait_ge(pick_step, PICKS * (e + 1))

            routed(0)
            pool.wait_ge(store_out[0], 32)
            pool.dma_start(U2B[0], u2_d[0:P, :]).then_inc(ctx_u2_in, 16)
            stretch(GROUPS, u=(0, 0))
            pool.wait_ge(rank_out, 1)
            pool.wait_ge(pick_in, 16)
            pool.wait_ge(u_free, HK + GROUP)
            stretch(GROUPS, v=(0, 0))
            pool.wait_ge(v_free, HK + GROUP)
            routed(1)
            stretch(GROUPS, u=(1, 0))
            routed(2)
            stretch(LAG, u=(2, 0))
            pool.wait_ge(q_done, 4 * TILES)
            for e in range(1, TILES):
                pool.wait_ge(rank_out, 2 * e + 1)
                more = e + 1 < TILES
                if not more:
                    last_sums()
                    break
                stretch(GROUPS - LAG, u=(e + 1, LAG), v=(e, 0))
                more = e + 2 < TILES
                if more:
                    routed(e + 2)
                stretch(LAG, u=(e + 2, 0) if more else None, v=(e, GROUPS - LAG))

        @block.tensor
        def _(pe):
            def ada(g):
                w = weights(pe, ("ada", g))
                if g >= 2:
                    pe.wait_ge(ada_out, g - 1)
                for k in range(KD):
                    j = k % 4
                    mm = pe.matmul(bank(6 + g % 2)[QUAD * j:QUAD * (j + 1), :], SILP[:, k, :], w[:, k, :],
                                   start=k < 4, stop=k >= 4, tile_position=(0, QUAD * j))
                mm.then_inc(ada_done, 1)

            def ada_sum(g):
                pe.wait_ge(ada_out, g + 1)
                if g >= 2:
                    pe.wait_ge(mod_added, mod_adds(g - 2))
                pe.matmul(bank(4 + g % 2)[0:2, :], SEL, PARTS4[g % 2], start=True, stop=True).then_inc(ada_summed, 1)

            def project(s, n):
                w = weights(pe, ("in", s, PROJ[n]))
                values = PROJ[n] == 5
                if s == 0:
                    i = n
                    if i >= 2:
                        pe.wait_ge(proj_out, i - 1)
                    for c in range(1 if values else 4):
                        for k in range(KD):
                            if n == 0:
                                pe.wait_ge(u_ready, 2 * (k + 1))
                            if values:
                                mm = pe.matmul(bank(i % 2), UT[:, k, 0:CTX], w[:, k, :], start=k == 0, stop=k == KD - 1)
                            else:
                                mm = pe.matmul(bank(i % 2)[:, c * P:(c + 1) * P], w[:, k, c * P:(c + 1) * P],
                                               UT[:, k, 0:CTX], start=k == 0, stop=k == KD - 1)
                    mm.then_inc(proj_done, 1)
                    return
                for c in range(4):
                    i = PROJ_AT[6 + n] + c
                    pe.wait_ge(proj_out, i - 1)
                    for k in range(KD):
                        if values:
                            mm = pe.matmul(bank(i % 2), UT[:, k, (c + 1) * P:(c + 2) * P], w[:, k, :],
                                           start=k == 0, stop=k == KD - 1)
                        else:
                            mm = pe.matmul(bank(i % 2), w[:, k, c * P:(c + 1) * P], UT[:, k, CTX:NT],
                                           start=k == 0, stop=k == KD - 1)
                    mm.then_inc(proj_done, 1)

            pe.wait_ge(silu_step, 3)
            pe.wait_ge(cond_in, 48)
            ada(0)
            for g in range(1, 4):
                ada(g)
                ada_sum(g - 1)
            ada_sum(3)
            pe.wait_ge(mod_added, 5)
            for m in range(16):
                mm = pe.transpose(bank(5)[:, 2 * m:2 * m + 2], MODS[:, m * P:(m + 1) * P], IDN[0:2, 0:2])
            mm.then_inc(modt_done, 1)
            for n in range(6):
                project(0, n)
                if 1 <= n <= 4:
                    ada_sum(2 + 2 * n)
                    ada_sum(3 + 2 * n)
                if n < 4:
                    ada(4 + 2 * n)
                    ada(5 + 2 * n)
            pe.wait_ge(proj_out, PROJ_CTX)
            pe.wait_ge(mod_added, mod_adds(11))
            for c in range(4):
                mm = pe.transpose(bank(4)[:, c * P:(c + 1) * P], Bk[:, c, 0:CTX], IDN)
            mm.then_inc(kt_done, 1)

            def scores(n):
                kind, a, j, par = UNITS[n]
                out = bank(n % 2)
                if n == 0:
                    pe.wait_ge(proj_out, PROJ_CTX)
                if n == 2:
                    pe.wait_ge(proj_out, PROJ_ALL)
                if n >= 2:
                    pe.wait_ge(s_scaled, n - 1)
                if n >= 4:
                    pe.wait_ge(win_step, 2 * (n - 3))
                if kind == "ctx":
                    for i in range(4):
                        p = slice(HD * a, HD * a + HD)
                        mm = pe.matmul(out[:, i * P:(i + 1) * P], Aq[p, i, 0:CTX], Bk[p, i, 0:CTX],
                                       start=True, stop=True)
                else:
                    if n == 2:
                        pe.wait_ge(ctx_in, 96)
                    p = slice(HD * par, HD * par + HD)
                    q = Aq[p, a, CTX + j * P:CTX + (j + 1) * P]
                    k = Bk[p, a, CTX:NT].rearrange("p (r c) -> p r c", c=GRID_W)[:, :, BAND_START[j]:BAND_START[j] + COL_BAND]
                    pe.matmul(out[:, 0:PAST].rearrange("p (r c) -> p r c", c=COL_BAND), q, k, start=True, stop=True)
                    mm = pe.matmul(bank(6 + n % 2)[:, 0:PAST], q, CK[p, a, :], start=True, stop=True)
                mm.then_inc(sc_done, 1)

            def turn(n):
                pe.wait_ge(norm_done, exps_upto(n))
                if n >= 2:
                    pe.wait_ge(pt_out, n - 1)
                for i in range(4):
                    mm = pe.transpose(bank(2 + n % 2)[:, i * P:(i + 1) * P], s_buf(n)[:, i * P:(i + 1) * P], IDN)
                mm.then_inc(pt_done, 1)

            def mix(n):
                kind, a, j, par = UNITS[n]
                o = out_block(n)
                pe.wait_ge(pt_out, n + 1)
                if o >= 2:
                    pe.wait_ge(po_out, o - 1)
                if n == 0:
                    pe.wait_ge(kt_out, 1)
                out = bank(4 + o % 2)
                if kind == "ctx":
                    for i in range(4):
                        h = 2 * i + a
                        mm = pe.matmul(out[HD * a:HD * a + HD, i * P:(i + 1) * P],
                                       V[0][:, 0, h * HD:(h + 1) * HD], pt_buf(n)[:, i * P:(i + 1) * P],
                                       start=True, stop=True)
                else:
                    if n == 2:
                        pe.wait_ge(band_in, 16 * BLOCKS * ROWS)
                    h = 2 * a + par
                    for i in range(4):
                        v = VB[:, 2 * j + i, h * HD:(h + 1) * HD] if i < 2 else CV[:, i - 2, h * HD:(h + 1) * HD]
                        mm = pe.matmul(out[HD * par:HD * par + HD, 0:P], v, pt_buf(n)[:, i * P:(i + 1) * P],
                                       start=i == 0, stop=i == 3)
                mm.then_inc(pv_done, 1)

            def attention(lo, hi):
                for n in range(lo, hi + 3):
                    if n < hi:
                        scores(n)
                    if lo + 2 <= n < hi + 2:
                        turn(n - 2)
                    if n >= lo + 3:
                        mix(n - 3)
                pe.wait_ge(po_out, outputs_upto(hi - 1))

            def rank_banks(e):
                return (4, 5) if e == 0 else (2, 3)

            def sum_banks(e):
                return bank(6 - 2 * (e % 2), 2)

            def rank_numbers(e):
                pe.wait_ge(pick_step, PICKS * (e + 1))
                if e >= 1:
                    pe.wait_ge(rank_out, 2 * e)
                pe.transpose(bank(rank_banks(e)[0])[:, 0:P], EIDF[e % 2], IDN).then_inc(rank_done, 1)

            def rank_weights(e):
                pe.wait_ge(weighed, e + 1)
                pe.transpose(bank(rank_banks(e)[1])[:, 0:P], WTOK, IDN).then_inc(rank_done, 1)

            def open_sums(e):
                y = sum_banks(e)
                if e >= 2:
                    pe.wait_ge(fin_step, FIN * (e - 2) + 1)
                for hf in range(2):
                    mm = pe.matmul(y[:, hf * HALF:(hf + 1) * HALF], ZERO[:, 0:P], ZERO, start=True, stop=False)
                if e == 0:
                    mm.then_inc(v_free, GROUP)

            def sum_groups(e, lo, hi):
                y = sum_banks(e)
                with pe.Fori(lo, hi) as g:
                    for b0 in (0, 4):
                        pe.wait_ge(cols_ready, 2 * g + (2 * GROUPS * e + b0 // 4 + 1))
                        for j in range(4):
                            pe.wait_ge(v_land[b0 + j], 16 * GROUPS * e + 16 * g + 16)
                        for hf in range(2):
                            for j in range(4):
                                mm = pe.matmul(y[QUAD * j:QUAD * (j + 1), hf * HALF:(hf + 1) * HALF],
                                               WCOL[b0 // 4][:, j, :], VR[e][b0 + j][:, hf * HALF:(hf + 1) * HALF],
                                               start=False, stop=False, tile_position=(0, QUAD * j))
                        mm.then_inc(v_free, 4)

            def last_groups(lo, hi):
                e = TILES - 1
                y = sum_banks(e)
                with pe.Fori(lo // 2, hi // 2) as g:
                    for k in range(4):
                        slots, land = (UR, u_land) if k < 2 else (VR[e], v_land)
                        done = 16 * GROUPS * (TILES if k < 2 else e)
                        b0 = 4 * (k % 2)
                        pe.wait_ge(cols_ready, 4 * g + (2 * GROUPS * e + k + 1))
                        for j in range(4):
                            pe.wait_ge(land[b0 + j], 16 * g + (done + 16))
                        for hf in range(2):
                            for j in range(4):
                                mm = pe.matmul(y[QUAD * j:QUAD * (j + 1), hf * HALF:(hf + 1) * HALF],
                                               LAST_COLS[k][:, j, :], slots[b0 + j][:, hf * HALF:(hf + 1) * HALF],
                                               start=False, stop=False, tile_position=(0, QUAD * j))
                        mm.then_inc(v_free, 4)

            def close_sums(e):
                y = sum_banks(e)
                for hf in range(2):
                    mm = pe.matmul(y[:, hf * HALF:(hf + 1) * HALF], ZERO[:, 0:P], ZERO, start=False, stop=True)
                mm.then_inc(y_done, 1)

            def section(s):
                t0, n_tok = SECTIONS[s]
                tok = slice(t0, t0 + n_tok)
                summed = [0]

                def context_sums(n):
                    sum_groups(0, summed[0], summed[0] + n)
                    summed[0] += n

                for hf in range(2):
                    for c in range(4):
                        d = 8 * s + 4 * hf + c
                        if d >= 1:
                            pe.wait_ge(sig_out, d)
                        col = slice(c * P, (c + 1) * P)
                        wc = merge_weights(pe, "gconv", s, hf, c)
                        for k in range(KD):
                            pe.matmul(bank(0)[:, 0:n_tok], wc[:, k, col], UT[:, k, tok], start=k == 0, stop=k == KD - 1)
                        wn = merge_weights(pe, "gna", s, hf, c)
                        for k in range(KD):
                            mm = pe.matmul(bank(1)[:, 0:n_tok], wn[:, k, col], UT[:, k, tok], start=k == 0,
                                           stop=k == KD - 1)
                        mm.then_inc(gates_done, 1)
                        if d >= 11:
                            context_sums(1)
                        if d >= 1:
                            pe.wait_ge(merge_step, 2 * d - 1)
                        wb = merge_weights(pe, "branch", s, hf, c)
                        for k in range(4):
                            pe.matmul(bank(2)[:, 0:n_tok], wb[:, k, col], Cy[:, k, tok], start=k == 0, stop=k == 3)
                        for k in range(4):
                            mm = pe.matmul(bank(3)[:, 0:n_tok], wb[:, 4 + k, col], YNA[s][:, k, :], start=k == 0,
                                           stop=k == 3)
                        mm.then_inc(merge_done, 1)
                        if d == 8:
                            rank_weights(0)
                        if 9 <= d < 15:
                            context_sums(1)
                pe.wait_ge(merge_step, 16 * (s + 1))
                tiles = (0,) if s == 0 else (1, 2, 3, 4)

                def turn_u2(e):
                    pe.wait_ge(ln_step, LNS * (e + 1))
                    if e >= 1:
                        pe.wait_ge(ut_out, e)
                    for k in range(KD):
                        mm = pe.transpose(bank(4, 2)[:, k * P:(k + 1) * P],
                                          U2[e][:, k * P:(k + 1) * P], IDN)
                    mm.then_inc(ut_done, 1)

                for e in tiles:
                    loc = slice((e - tiles[0]) * P, (e - tiles[0] + 1) * P)
                    if e >= 3:
                        pe.wait_ge(ln_step, LNS * (e - 2) + 1)
                    for hf in range(2):
                        w = weights(pe, ("out", s, hf))
                        for k in range(KD):
                            mm = pe.matmul(bank(2 * (e % 2) + hf), MT[s][:, k, loc], w[:, k, :], start=k == 0,
                                           stop=k == KD - 1)
                    mm.then_inc(wo_done, 1)
                    if e > tiles[0]:
                        turn_u2(e - 1)
                    if s == 1 and e < tiles[-1]:
                        context_sums(1)
                if s == 0:
                    turn_u2(0)
                else:
                    pe.wait_ge(ln_step, LNS * tiles[-1] + 1)
                pe.wait_ge(keys_in, 16)
                def key_scores(i):
                    pe.wait_ge(q_out, i + 1)
                    if i >= 2:
                        if (i - 2) // 4 in SUMMED_LATE:
                            pe.wait_ge(ss_out, i - 1 - 4 * SUMMED_LATE[0])
                        else:
                            pe.wait_ge(topk_step, 20 * (i - 1))
                    for c in range(4):
                        mm = pe.matmul(bank(2 + i % 2)[:, c * P:(c + 1) * P], QT[s][i % 2][:, c, :],
                                       SK[:, 4 * (i % 4) + c, :], start=True, stop=True)
                    mm.then_inc(ss_done, 1)

                for i in range(4 * tiles[0], 4 * tiles[-1] + 4):
                    e, qg = divmod(i, 4)
                    w = weights(pe, ("query", s, qg))
                    pe.wait_ge(ut_out, e + 1)
                    if i >= 2:
                        pe.wait_ge(q_out, i - 1)
                    for c in range(4):
                        for k in range(KD):
                            mm = pe.matmul(bank(i % 2)[:, c * P:(c + 1) * P], w[:, k, c * P:(c + 1) * P],
                                           UT[:, k, e * P:(e + 1) * P], start=k == 0, stop=k == KD - 1)
                    mm.then_inc(q_done, 1)
                    if i == 4:
                        turn_u2(tiles[-1])
                    if i > 4 * tiles[0]:
                        key_scores(i - 1)
                    if i in (4, 5):
                        context_sums(1)
                    if i == 5:
                        close_sums(0)
                key_scores(4 * tiles[-1] + 3)
                assert s == 0 or summed[0] == GROUPS

            attention(0, 2)
            section(0)
            for n in range(6):
                project(1, n)
            attention(2, NU)
            rank_numbers(0)
            open_sums(0)
            section(1)
            pe.wait_ge(ss_out, 4 * len(SUMMED_LATE))
            rank_numbers(1)
            rank_weights(1)
            for e in range(1, TILES):
                open_sums(e)
                if e + 1 < TILES:
                    sum_groups(e, 0, GROUPS - 1)
                    rank_numbers(e + 1)
                    rank_weights(e + 1)
                    sum_groups(e, GROUPS - 1, GROUPS)
                else:
                    last_groups(0, GROUPS)
                close_sums(e)

        @block.scalar
        def _(act):
            for dst, src in ((CT2, c_T), (SEL, sel_in), (IDN, ident_in)):
                act.dma_start(dst, src).then_inc(cond_in, 16)
            act.wait_ge(cond_in, 48)
            act.activation(SIL, CT2, ACT.Sigmoid).then_inc(silu_step, 1)

            def take_partial(g):
                act.wait_ge(ada_done, g + 1)
                if g >= 2:
                    act.wait_ge(ada_summed, g - 1)
                act.activation(PARTS4[g % 2], bank(6 + g % 2), ACT.Copy).then_inc(ada_out, 1)

            for g in range(4):
                take_partial(g)
            for i in range(PROJ_CTX):
                if 1 <= i <= 4:
                    take_partial(2 + 2 * i)
                    take_partial(3 + 2 * i)
                act.wait_ge(proj_done, i + 1)
                if i == 4:
                    act.wait_ge(conv_step, 14)
                if PROJ[i] == 5:
                    dst, src = V[0][:, 0, :], bank(i % 2)
                else:
                    dst = {0: Aq, 2: Bk, 1: Cy, 3: Aq, 4: Bk}[PROJ[i]][:, :, 0:CTX]
                    src = bank(i % 2).rearrange("p (c t) -> p c t", t=P)
                act.activation(dst, src, ACT.Copy).then_inc(proj_out, 1)

            def take_projection():
                for i in range(PROJ_CTX, PROJ_ALL):
                    n, c = divmod(i - PROJ_CTX, 4)
                    act.wait_ge(proj_done, i + 1)
                    if i == PROJ_AT[6 + 4]:
                        act.wait_ge(conv_step, 28)
                    src = bank(i % 2)
                    if PROJ[n] == 5:
                        dst = V[1][:, c, :]
                    else:
                        dst = {0: Aq, 2: Bk, 1: Cy, 3: Aq, 4: Bk}[PROJ[n]][:, c, CTX:NT]
                    if PROJ[n] == 3:
                        dst = dst.rearrange("p (j r c) -> p r j c", j=BLOCKS, r=ROWS)
                        src = src.rearrange("p (r j c) -> p r j c", j=BLOCKS, c=COL_BLOCK)
                    act.activation(dst, src, ACT.Copy).then_inc(proj_out, 1)
                    if i == PROJ_CTX + 2:
                        gate_exponents(0)

            act.wait_ge(kt_done, 1)
            act.activation(KTOK, bank(4), ACT.Copy).then_inc(kt_out, 1)

            def scale(n):
                act.wait_ge(sc_done, n + 1)
                if n >= 3:
                    act.wait_ge(pt_done, n - 2)
                if UNITS[n][0] == "ctx":
                    dst, src = s_buf(n), bank(n % 2)
                else:
                    dst, src = s_buf(n)[:, PAST:HALF], bank(6 + n % 2)[:, 0:PAST]
                act.activation(dst, src, ACT.Copy, scale=SCALE).then_inc(s_scaled, 1)

            def exponents(n):
                act.wait_ge(max_done, n + 1)
                parts = 4 if UNITS[n][0] == "ctx" else 1
                for i in range(parts):
                    v = s_buf(n)[:, i * (HALF // parts):(i + 1) * (HALF // parts)]
                    act.activation(v, v, ACT.Exp, bias=NMAX[:, n % 3, i:i + 1], accum_out=RSUM[:, n % 3, i:i + 1]
                                   ).then_inc(exp_done, 1)

            def take_turned(n):
                act.wait_ge(pt_done, n + 1)
                if n >= 2:
                    act.wait_ge(pv_done, n - 1)
                act.activation(pt_buf(n), bank(2 + n % 2), ACT.Copy).then_inc(pt_out, 1)

            def take_out(n):
                kind, a, j, par = UNITS[n]
                if kind == "lat" and par == 0:
                    return
                act.wait_ge(pv_done, n + 1)
                src = bank(4 + out_block(n) % 2)
                if kind == "ctx":
                    own = slice(HD * a, HD * a + HD)
                    act.activation(YNA[0][own], src[own].rearrange("p (a b) -> p a b", a=4),
                                   ACT.Copy).then_inc(po_out, 1)
                else:
                    dst = YNA[1][:, a, :].rearrange("p (r c) -> p r c", c=GRID_W)[:, :, j * COL_BLOCK:(j + 1) * COL_BLOCK]
                    act.activation(dst, src[:, 0:P].rearrange("p (r c) -> p r c", c=COL_BLOCK), ACT.Copy
                                   ).then_inc(po_out, 1)

            def gate_exponents(e):
                act.wait_ge(pick_step, PICKS * e + SUB_AT)
                act.activation(SMAX, SMAX, ACT.Exp).then_inc(gexp_done, 1)

            def attention(lo, hi):
                for n in range(lo, hi + 3):
                    if n < hi:
                        scale(n)
                    if lo < n <= hi:
                        exponents(n - 1)
                    if lo + 2 <= n <= hi + 1:
                        take_turned(n - 2)
                    if n >= lo + 3:
                        take_out(n - 3)

            def weigh(e):
                act.wait_ge(dots_out, GROUPS * (e + 1))
                if e >= 1:
                    act.wait_ge(rank_done, 2 * e)
                act.activation(WTOK, DOTS[e % 2], ACT.Gelu).then_inc(gelu_done, 1)

            def take_rank(e, n):
                dst, b = ((EIDT, WT)[n][e % 2], (4 if e == 0 else 2) + n)
                act.wait_ge(rank_done, 2 * e + n + 1)
                if e >= 2:
                    act.wait_ge(v_free, HK * (e - 1) + GROUP)
                act.activation(dst.rearrange("p (i j) -> p j i", j=4),
                               bank(b)[:, 0:P].rearrange("p (j i) -> p j i", j=4), ACT.Copy).then_inc(rank_out, 1)

            def load_x(e):
                act.dma_start(XB[min(e, 1)], rows(x_prompt, x_sample, e)).then_inc(xb_in, 16)

            def section(s):
                t0, n_tok = SECTIONS[s]
                if s == 0:
                    act.wait_ge(mods_out, 16)
                else:
                    act.wait_ge(win_step, 2 * (NU - 2))
                own = mods_d[s:s + 1, :]
                for n, row in ((0, own[:, 2 * D:3 * D]), (1, ln1_g[0:1, :]), (2, ln1_b[0:1, :]),
                               (3, own[:, 4 * D:5 * D]), (4, own[:, 3 * D:4 * D])):
                    act.dma_start(PRM[s][n], row.partition_broadcast(P)).then_inc(prm_in[s], 16)
                for i in range(8):
                    d = 8 * s + i
                    act.wait_ge(gates_done, d + 1)
                    if d >= 1:
                        act.wait_ge(merge_step, 2 * d)
                    src = bank(0, 2).rearrange("p (a b) -> p a b", a=2)[:, :, 0:n_tok]
                    act.activation(SG[s], src, ACT.Sigmoid).then_inc(sig_out, 1)
                    if d == 8:
                        take_rank(0, 1)
                if s == 0:
                    act.wait_ge(cache_out, 32)
                load_x(s)
                tiles = (0,) if s == 0 else (1, 2, 3, 4)
                for e in tiles:
                    act.wait_ge(ln_step, LNS * e + 6)
                    act.activation(RSTD[:, 0:1], MV[:, 1:2], ACT.Sqrt).then_inc(sqrt_done, 1)
                    if e + 1 in tiles:
                        load_x(e + 1)
                    act.wait_ge(ut_done, e + 1)
                    act.activation(UT[:, :, e * P:(e + 1) * P], bank(4, 2).rearrange("p (k t) -> p k t", t=P),
                                   ACT.Copy).then_inc(ut_out, 1)
                    act.wait_ge(ln_step, LNS * (e + 1))
                    act.dma_start(x1_d[e * P:(e + 1) * P, :], XR[e]).then_inc(store_out[e % 2], 16)
                    act.dma_start(u2_d[e * P:(e + 1) * P, :], U2[e]).then_inc(store_out[e % 2], 16)

                def keep_scores(i):
                    if i // 4 in SUMMED_LATE:
                        act.wait_ge(ss_done, i + 1)
                        act.activation(LATE[i // 4][:, i % 4, :], bank(2 + i % 2), ACT.Copy).then_inc(ss_out, 1)

                for i in range(4 * tiles[0], 4 * tiles[-1] + 4):
                    act.wait_ge(q_done, i + 1)
                    if i >= 2:
                        act.wait_ge(ss_done, i - 1)
                    act.activation(QT[s][i % 2], bank(i % 2).rearrange("p (c t) -> p c t", t=P), ACT.Copy
                                   ).then_inc(q_out, 1)
                    keep_scores(i - 1)
                    if i == 9:
                        gate_exponents(1)
                keep_scores(4 * tiles[-1] + 3)

            def deviation(e):
                act.wait_ge(fin_step, FIN * e + 6)
                act.activation(RSTD[:, 0:1], MV[:, 1:2], ACT.Sqrt).then_inc(fsqrt_done, 1)

            attention(0, 2)
            section(0)
            take_projection()
            attention(2, NU)
            take_rank(0, 0)
            weigh(0)
            section(1)
            for e in range(1, TILES):
                for old in FINISHED_IN[e]:
                    deviation(old)
                if e + 1 < TILES:
                    gate_exponents(e + 1)
                weigh(e)
                take_rank(e, 0)
                take_rank(e, 1)
            for e in FINISHED_IN[TILES]:
                deviation(e)

        @block.vector
        def _(dve):
            def layer_norm(step, base, out, gain, shift, sqrt_sem, sqrt_count):
                for hf in range(2):
                    dve.bn_stats(STAT[:, 6 * hf:6 * hf + 6], out[:, hf * HALF:(hf + 1) * HALF]).then_inc(step, 1)
                dve.wait_ge(step, base + 2)
                dve.bn_aggr(MV, STAT).then_inc(step, 1)
                dve.wait_ge(step, base + 3)
                dve.tensor_scalar(MV[:, 1:2], MV[:, 1:2], EPS, None, ALU.add).then_inc(step, 1)
                dve.wait_ge(sqrt_sem, sqrt_count)
                dve.reciprocal(RSTD[:, 1:2], RSTD[:, 0:1]).then_inc(step, 1)
                dve.wait_ge(step, base + 5)
                dve.tensor_scalar(out, out, MV[:, 0:1], RSTD[:, 1:2], ALU.subtract, ALU.mult).then_inc(step, 1)
                dve.wait_ge(step, base + 6)
                dve.tensor_tensor(out, out, gain, ALU.mult).then_inc(step, 1)
                dve.wait_ge(step, base + 7)
                dve.tensor_tensor(out, out, shift, ALU.add).then_inc(step, 1)

            dve.memset(ZERO, 0.0).then_inc(zero_set, 1)
            dve.memset(SILP, 0.0).then_inc(silu_step, 1)
            dve.wait_ge(silu_step, 2)
            dve.tensor_tensor(SILP[:, :, 0:2], SIL, CT2, ALU.mult).then_inc(silu_step, 1)
            dve.wait_ge(bada_in, 16)

            def add_mods(g):
                dve.wait_ge(ada_summed, g + 1)
                own = MODS[:, g * HALF:(g + 1) * HALF]
                dve.tensor_tensor(own, own, bank(4 + g % 2)[0:2, :], ALU.add).then_inc(mod_added, 1)

            for g in range(4):
                add_mods(g)
            dve.wait_ge(mod_added, 4)
            dve.tensor_scalar(MODS[:, D:2 * D], MODS[:, D:2 * D], 1.0, None, ALU.add).then_inc(mod_added, 1)
            dve.wait_ge(modt_done, 1)
            dve.tensor_copy(MODT, bank(5)[:, 0:32].rearrange("p (a b) -> p a b", b=2)).then_inc(modt_ready, 1)
            dve.wait_ge(modt_ready, 1)
            dve.wait_ge(x_in, 16 * KD)
            for k in range(KD):
                for s, (t0, n_tok) in enumerate(SECTIONS):
                    v = UT[:, k, t0:t0 + n_tok]
                    dve.tensor_scalar(v, v, MODT[:, KD + k, s:s + 1], MODT[:, k, s:s + 1], ALU.mult, ALU.add
                                      ).then_inc(u_ready, 1)
            for g in range(4, 8):
                add_mods(g)
            def convolve(s):
                (t0, n_tok), base, ct = SECTIONS[s], 14 * s, CT[s]
                own = slice(t0, t0 + n_tok)
                dve.wait_ge(proj_out, PROJ_AT[6 * s + 3])
                dve.tensor_tensor(Aq[:, :, own], Aq[:, :, own], Bk[:, :, own], ALU.mult).then_inc(conv_step, 1)
                dve.wait_ge(conv_step, base + 1)
                for c in range(4):
                    dve.tensor_scalar(ct[:, c, :], Aq[:, c, own], CONVW[:, c, 1:2], None, ALU.mult).then_inc(conv_step, 1)
                dve.wait_ge(conv_step, base + 5)
                for c in range(4):
                    o = ct[:, c, 1:n_tok]
                    dve.scalar_tensor_tensor(o, Aq[:, c, t0:t0 + n_tok - 1], CONVW[:, c, 0:1], o, ALU.mult, ALU.add
                                             ).then_inc(conv_step, 1)
                dve.wait_ge(conv_step, base + 9)
                for c in range(4):
                    o = ct[:, c, 0:n_tok - 1]
                    dve.scalar_tensor_tensor(o, Aq[:, c, t0 + 1:t0 + n_tok], CONVW[:, c, 2:3], o, ALU.mult, ALU.add
                                             ).then_inc(conv_step, 1)
                dve.wait_ge(conv_step, base + 13)
                dve.tensor_tensor(Cy[:, :, own], Cy[:, :, own], ct, ALU.mult).then_inc(conv_step, 1)

            dve.wait_ge(consts_in, 48)
            convolve(0)
            for g in range(8, 12):
                add_mods(g)
            dve.wait_ge(mod_added, 13)
            dve.tensor_scalar(MODS[:, 4 * D:5 * D], MODS[:, 4 * D:5 * D], 1.0, None, ALU.add).then_inc(mod_added, 1)

            def window(n):
                kind, a, j, par = UNITS[n]
                if kind == "lat":
                    if n == 2:
                        dve.wait_ge(bias_in, 16 * ROWS * HEADS)
                    dve.wait_ge(sc_done, n + 1)
                    if n >= 3:
                        dve.wait_ge(pt_done, n - 2)
                    h = 2 * a + par
                    off = BAND_START[j] - j * COL_BLOCK + COL_BLOCK
                    v = s_buf(n)[:, 0:PAST].rearrange("p (r c) -> p r c", c=COL_BAND)
                    dve.scalar_tensor_tensor(v, bank(n % 2)[:, 0:PAST].rearrange("p (r c) -> p r c", c=COL_BAND), SCALE,
                                             WB[:, h, :, off:off + COL_BAND], ALU.mult, ALU.add).then_inc(win_step, 1)
                    dve.wait_ge(win_step, 2 * (n - 2) + 1)
                    mask = MASK[:, MASK_OF[j]:MASK_OF[j] + 1, :].to_broadcast([P, ROWS, COL_BAND])
                    dve.tensor_tensor(v, v, mask, ALU.add).then_inc(win_step, 1)
                    dve.wait_ge(win_step, 2 * (n - 1))
                dve.wait_ge(s_scaled, n + 1)
                parts = 4 if kind == "ctx" else 1
                dve.tensor_reduce(NMAX[:, n % 3, 0:parts], s_buf(n).rearrange("p (a b) -> p a b", a=parts), AX, ALU.max,
                                  negate=True).then_inc(max_done, 1)

            def normalise(n):
                parts = 4 if UNITS[n][0] == "ctx" else 1
                dve.wait_ge(exp_done, exps_upto(n))
                dve.reciprocal(RINV[:, n % 3, 0:parts], RSUM[:, n % 3, 0:parts]).then_inc(recip_done, 1)
                dve.wait_ge(recip_done, n + 1)
                for i in range(parts):
                    v = s_buf(n)[:, i * (HALF // parts):(i + 1) * (HALF // parts)]
                    dve.tensor_scalar(v, v, RINV[:, n % 3, i:i + 1], None, ALU.mult).then_inc(norm_done, 1)

            def dot_products(e, g, b0, n):
                for b in range(b0, b0 + n):
                    dve.wait_ge(u_land[b], 16 * GROUPS * e + 16 * g + 16)
                    dve.tensor_tensor_reduce(UR[b], UR[b], U2B[e], 1.0, 0.0, ALU.mult, ALU.add,
                                             DOT[:, b:b + 1]).then_inc(u_free, 1)

            def keep_dots(e, g):
                dve.wait_ge(u_free, GROUP * g + (HK * e + 2 * GROUP))
                dve.tensor_copy(DOTS[e % 2][:, bass.ds(GROUP * g, GROUP)], DOT).then_inc(dots_out, 1)
                dve.wait_ge(dots_out, GROUPS * e + g + 1)

            def attention(lo, hi):
                for n in range(lo, hi + 1):
                    if n < hi:
                        window(n)
                    if n > lo:
                        normalise(n - 1)
                    g, part = CTX_GROUPS[1] + (n - 2) // 4, (n - 2) % 4
                    if lo == 2 and n < hi and g < GROUPS:
                        dot_products(0, g, 2 * part, 2)
                        if part == 3:
                            keep_dots(0, g)

            def route(e, part):
                base = PICKS * e
                val = VAL[e].rearrange("p (h s k) -> p h s k", s=2, k=TOPK)
                idxf = IDXF.rearrange("p (h s k) -> p h s k", s=2, k=TOPK)
                cube = [P, PEER_HEADS, TOPK, TOPK]
                if part == 0:
                    dve.wait_ge(topk_step, 80 * (e + 1))
                if part or e:
                    dve.wait_ge(pick_step, base + ROUTE_AT[part])
                step = [base + ROUTE_AT[part]]

                def done(ins):
                    step[0] += 1
                    ins.then_inc(pick_step, 1)

                def settle():
                    dve.wait_ge(pick_step, step[0])

                cands = CANDS[e].rearrange("p h (a b) -> p h a b", b=TOPK)
                eq = EQ[e].rearrange("p h (a b) -> p h a b", b=TOPK)
                pos = POS.rearrange("p (h k) -> p h k", k=TOPK)
                smax = SMAX.rearrange("p (h k) -> p h k", k=TOPK)
                iota = IOTA.unsqueeze(1).unsqueeze(1).to_broadcast(cube)
                digits = (AF, BF)

                def best(lo):
                    for h in range(PEER_HEADS):
                        done(dve.max(TOPS[:, h, lo:lo + 8], CANDS[e][:, h, :]))

                def places(lo):
                    for h in range(PEER_HEADS):
                        done(dve.max_index(pos[:, h, lo:lo + 8], TOPS[:, h, lo:lo + 8], CANDS[e][:, h, :]))

                def key_numbers(side):
                    digit = digits[side].rearrange("p (h k) -> p h k", k=TOPK)
                    done(dve.tensor_tensor(eq, digit.unsqueeze(3).to_broadcast(cube), iota, ALU.is_equal))
                    settle()
                    done(dve.tensor_tensor(eq, eq, idxf[:, :, side, :].unsqueeze(2).to_broadcast(cube), ALU.mult))
                    settle()
                    done(dve.tensor_reduce(digit, eq, AX, ALU.add))

                if part == 0:
                    done(dve.tensor_tensor(cands, val[:, :, 0, :].unsqueeze(3).to_broadcast(cube),
                                           val[:, :, 1, :].unsqueeze(2).to_broadcast(cube), ALU.add))
                    done(dve.tensor_copy(IDXF, IDXS[e]))
                    settle()
                    best(0)
                elif part == 1:
                    places(0)
                    settle()
                    for h in range(PEER_HEADS):
                        done(dve.match_replace(CANDS[e][:, h, :], TOPS[:, h, 0:8], CANDS[e][:, h, :], LOWEST))
                elif part == 2:
                    best(8)
                    settle()
                    places(8)
                    done(dve.tensor_tensor(smax, TOPS, TOPS[:, :, 0:1].to_broadcast([P, PEER_HEADS, TOPK]), ALU.subtract))
                elif part == 3:
                    done(dve.tensor_scalar(PA, POS, 4, None, ALU.logical_shift_right))
                    done(dve.tensor_scalar(POS, POS, TOPK - 1, None, ALU.bitwise_and))
                    settle()
                    done(dve.tensor_copy(AF, PA))
                    done(dve.tensor_copy(BF, POS))
                    settle()
                    key_numbers(0)
                elif part == 4:
                    key_numbers(1)
                else:
                    done(dve.scalar_tensor_tensor(EID[e % 2], AF, float(NKEYS), BF, ALU.mult, ALU.add))
                    if e >= 2:
                        dve.wait_ge(rank_done, 2 * e - 3)
                    done(dve.scalar_tensor_tensor(EIDF[e % 2], AF, float(NKEYS), BF, ALU.mult, ALU.add))
                    dve.wait_ge(gexp_done, e + 1)
                    done(dve.tensor_reduce(GSUM, smax, AX, ALU.add))
                    settle()
                    done(dve.reciprocal(GSUM, GSUM))
                    settle()
                    done(dve.tensor_tensor(GATE[e % 2].rearrange("p (h k) -> p h k", k=TOPK), smax,
                                           GSUM.unsqueeze(2).to_broadcast([P, PEER_HEADS, TOPK]), ALU.mult))
                assert step[0] == base + ROUTE_AT[part + 1], (part, step[0] - base)

            def section(s):
                n_tok = SECTIONS[s][1]
                tiles = (0,) if s == 0 else (1, 2, 3, 4)
                for i in range(8):
                    d = 8 * s + i
                    sg = SG[s]
                    dve.wait_ge(sig_out, d + 1)
                    dve.wait_ge(merge_done, d + 1)
                    dve.tensor_tensor(sg, sg, bank(2, 2).rearrange("p (a b) -> p a b", a=2)[:, :, 0:n_tok],
                                      ALU.mult).then_inc(merge_step, 1)
                    dve.wait_ge(merge_step, 2 * d + 1)
                    dve.tensor_tensor(MT[s][:, i, :], sg[:, 0, :], sg[:, 1, :], ALU.add).then_inc(merge_step, 1)
                for e in tiles:
                    base = LNS * e
                    xr, xb, u2 = XR[e], XB[s], U2[e]
                    dve.wait_ge(wo_done, e + 1)
                    dve.wait_ge(prm_in[s], 80)
                    dve.wait_ge(xb_in, 16 * (e + 1))
                    if e >= 3:
                        dve.wait_ge(store_out[e % 2], 32 * (e // 2))
                    dve.tensor_tensor(xr, bank(2 * (e % 2), 2), PRM[s][0], ALU.mult).then_inc(ln_step, 1)
                    dve.wait_ge(ln_step, base + 1)
                    dve.scalar_tensor_tensor(xr, xb, ALPHA, xr, ALU.mult, ALU.add).then_inc(ln_step, 1)
                    dve.wait_ge(ln_step, base + 2)
                    layer_norm(ln_step, base + 2, xr, PRM[s][1], PRM[s][2], sqrt_done, e + 1)
                    dve.wait_ge(ln_step, base + 10)
                    dve.tensor_tensor(u2, xr, PRM[s][3], ALU.mult).then_inc(ln_step, 1)
                    dve.wait_ge(ln_step, base + 11)
                    dve.tensor_tensor(u2, u2, PRM[s][4], ALU.add).then_inc(ln_step, 1)

            def rank_keys(e, qg):
                si = 4 * e + qg
                idx = IDXS[e]
                if e not in SUMMED_LATE:
                    dve.wait_ge(ss_done, si + 1)
                else:
                    dve.wait_ge(ss_out, si + 1 - 4 * SUMMED_LATE[0])
                if si >= 1:
                    dve.wait_ge(topk_step, 20 * si)
                sc = LATE[e][:, qg, :] if e in SUMMED_LATE else bank(2 + si % 2)

                def best(c, lo):
                    o = (4 * qg + c) * TOPK + lo
                    return slice(o, o + 8)

                for lo in (0, 8):
                    for c in range(4):
                        src = sc[:, c * P:(c + 1) * P] if lo == 0 else SW[:, c, :]
                        dve.max(VAL[e][:, best(c, lo)], src).then_inc(topk_step, 1)
                    dve.wait_ge(topk_step, 20 * si + 4 + 12 * (lo // 8))
                    for c in range(4):
                        src = sc[:, c * P:(c + 1) * P] if lo == 0 else SW[:, c, :]
                        dve.max_index(idx[:, best(c, lo)], VAL[e][:, best(c, lo)], src).then_inc(topk_step, 1)
                    if lo == 0:
                        for c in range(4):
                            dve.match_replace(SW[:, c, :], VAL[e][:, best(c, 0)], sc[:, c * P:(c + 1) * P], LOWEST
                                              ).then_inc(topk_step, 1)
                        dve.wait_ge(topk_step, 20 * si + 12)

            def finish(e):
                base = FIN * e
                yr = YR[e % 2]
                dve.wait_ge(y_done, e + 1)
                dve.wait_ge(prm2_in, 48 if e == 0 else 64)
                dve.wait_ge(x1_in[e % 2], 16 * (e // 2 + 1))
                if e >= 2:
                    dve.wait_ge(y_out[e % 2], 16 * (e // 2))
                dve.tensor_tensor(yr, bank(6 - 2 * (e % 2), 2), PRM2[0], ALU.mult).then_inc(fin_step, 1)
                dve.wait_ge(fin_step, base + 1)
                dve.scalar_tensor_tensor(yr, X1B[e % 2], ALPHA, yr, ALU.mult, ALU.add).then_inc(fin_step, 1)
                dve.wait_ge(fin_step, base + 2)
                layer_norm(fin_step, base + 2, yr, PRM2[1], PRM2[2], fsqrt_done, e + 1)

            def groups(e, lo, hi):
                if lo == hi:
                    return
                with dve.Fori(lo, hi) as g:
                    dot_products(e, g, 0, GROUP)
                    keep_dots(e, g)

            def weigh(e):
                dve.wait_ge(gelu_done, e + 1)
                dve.tensor_tensor(WTOK, WTOK, GATE[e % 2], ALU.mult).then_inc(weighed, 1)

            def choose(e):
                for qg in range(4):
                    rank_keys(e, qg)
                for part in range(PARTS):
                    route(e, part)

            attention(0, 2)
            section(0)
            choose(0)
            dve.memset(DOT, 0.0).then_inc(u_free, GROUP)
            dve.wait_ge(u_free, GROUP)
            dve.wait_ge(ctx_u2_in, 16)
            groups(0, 0, CTX_GROUPS[0])
            convolve(1)
            groups(0, *CTX_GROUPS)
            attention(2, NU)
            groups(0, CTX_GROUPS[1] + (NU - 2) // 4, GROUPS)
            weigh(0)
            section(1)
            all_stored(dve)
            choose(1)
            for e in range(1, TILES):
                work = [(1 + qg, rank_keys, 2, qg) for qg in range(4)] if e == 1 else []
                if e == 2:
                    work += [(3 + qg, rank_keys, 3, qg) for qg in range(4)]
                if e + 1 < TILES:
                    work += [(6 + part, route, e + 1, part) for part in range(PARTS)]
                if e == 2:
                    work += [(12 + qg, rank_keys, 4, qg) for qg in range(4)]
                dve.wait_ge(u2_in[e % 2], 16 * ((e + 1) // 2))
                g = 0
                if FINISHED_IN[e]:
                    g = 4 if e > 2 else 2
                    groups(e, 0, g)
                    finish(FINISHED_IN[e][0])
                for at_group, do, tile, part in work:
                    groups(e, g, at_group)
                    do(tile, part)
                    g = at_group
                groups(e, g, GROUPS)
                weigh(e)
            for e in FINISHED_IN[TILES]:
                finish(e)


FINISHED_IN = {1: (), 2: (0,), 3: (1,), 4: (2,), 5: (3, 4)}
LNS = 12
FIN = 10
SUB_AT = 2 + 5 * PEER_HEADS + 1
ROUTE_AT = (0, 2 + PEER_HEADS, 2 + 3 * PEER_HEADS, SUB_AT, SUB_AT + 7, SUB_AT + 10, SUB_AT + 15)
PARTS = len(ROUTE_AT) - 1
PICKS = ROUTE_AT[-1]
CTX_GROUPS = (4, 7)

_OUTS = [((1, CTX, D), "y_prompt"), ((1, LAT, D), "y_sample"), ((1, 1, CTX, HEADS, HD), "new_k"),
         ((1, 1, CTX, HEADS, HD), "new_v")]


def kernel(**inputs):
    import numpy as _np
    import concourse.bacc as _bacc
    from concourse import mybir as _mybir
    from concourse.bass_utils import run_bass_kernel_spmd as _run

    i = {k: _np.asarray(v) for k, v in inputs.items()}
    xs = _np.concatenate([i["x_prompt"][0], i["x_sample"][0]], axis=0)
    rpb = _np.pad(i["rpb"].reshape(-1), (16, 16))
    laid = {
        "x_prompt": i["x_prompt"], "x_sample": i["x_sample"], "xT": xs.T,
        "ck_T": i["cache_k"][0, 0].reshape(PAST, HEADS * HD).T, "cache_v": i["cache_v"],
        "c_T": _np.stack([i["c_ctx"], i["c"][0]], axis=-1).reshape(KD, P, 2).transpose(1, 0, 2),
        "w_ada": i["w_ada"], "b_ada": i["b_ada"], "w_in": i["w_in"],
        "convw_T": i["conv_w"][0].reshape(3, 4, P).transpose(2, 1, 0),
        "w_conv_out": i["w_conv_out"], "w_na_out": i["w_na_out"],
        "rpb_rows": _np.stack([rpb[15 - q:15 - q + rpb.size - 15] for q in range(COL_BLOCK)]),
        "w_o": i["w_o"], "ln1_g": i["ln1_g"], "ln1_b": i["ln1_b"], "w_query": i["w_query"],
        "sub_keys_T": i["sub_keys"][0].reshape(2 * PEER_HEADS, NKEYS, P).transpose(2, 0, 1),
        "expert_u": i["expert_u"], "expert_v": i["expert_v"], "ln2_g": i["ln2_g"], "ln2_b": i["ln2_b"],
        "ident_in": _np.eye(P, dtype=_np.float32),
        "sel_in": _np.tile(_np.eye(QUAD, 2, dtype=_np.float32), (4, 1)), "mask_in": window_mask(),
        "iota_in": _np.tile(_np.arange(TOPK, dtype=_np.float32), (P, 1)),
        "pickrow_in": _np.eye(QUAD, dtype=_np.float32).reshape(1, QUAD, QUAD),
    }
    nc = _bacc.Bacc("TRN2", target_bir_lowering=False, num_devices=1)
    arrays, args = {}, []
    for name, a in laid.items():
        a = _np.ascontiguousarray(a)
        arrays[f"in_{name}_dram"] = a
        args.append(nc.dram_tensor(f"in_{name}_dram", a.shape, _mybir.dt.from_np(a.dtype), kind="ExternalInput").ap())
    for shape, name in _OUTS:
        args.append(nc.dram_tensor(f"out_{name}_dram", shape, F32, kind="ExternalOutput").ap())
    backbone(nc, *args)
    r = _run(nc, [arrays], core_ids=[0])
    return tuple(r.results[0][f"out_{name}_dram"] for _, name in _OUTS)
```
